# Optimizing a Trainium2 kernel written in Bass

```python
import jax, jax.numpy as jnp
from jax import lax
import numpy as np

D_MODEL = 1024
BATCH = 1
SEQ = 256
DEPTH = 1

N_MEM = 256
ATT_HEADS = 8
ATT_HD = 64
ATT_W = ATT_HEADS * ATT_HD
IDX_HEADS = 4
IDX_HD = 64
TOPK_MAX = 256
Q_BLOCK = 128
RWKV_HEADS = 8
RWKV_HD = 64
RWKV_W = RWKV_HEADS * RWKV_HD
DECAY_LORA = 64
AAA_LORA = 64
GATE_LORA = 128
GN_EPS = 64e-5
MEM_HEADS = 4
MEM_HD = 128
MEM_W = MEM_HEADS * MEM_HD
N_BRANCH = 3
BRANCH_W = 512
ROPE_THETA = 500000.0
ROPE_FRACTION = 4
NORM_EPS = 1e-6
PEER_KEYS = 128
N_EXPERTS = PEER_KEYS * PEER_KEYS
PEER_HEADS = 8
PEER_QDIM = 256
PEER_TOPK = 16
PEER_BLOCK = 128

ATT_IN = 3 * ATT_W + IDX_HEADS * IDX_HD + IDX_HD + IDX_HEADS
RWKV_IN = 3 * RWKV_W + DECAY_LORA + AAA_LORA + GATE_LORA
GATE_IN = N_BRANCH * D_MODEL
W_IN_COLS = ATT_IN + RWKV_IN + MEM_W + GATE_IN

kernel_name = 'dsa_rwkv7_memory_gated_peer_layer'

F32 = jnp.float32

def split_last(t, sizes):
    offs = np.cumsum(sizes)[:-1].tolist()
    return jnp.split(t, offs, axis=-1)

def rmsnorm(t, gain):
    tf = t.astype(F32)
    out = tf * lax.rsqrt(jnp.mean(tf * tf, axis=-1, keepdims=True) + NORM_EPS) * gain.astype(F32)
    return out.astype(t.dtype)

def rope_tables(positions, head_dim):
    rot = head_dim // ROPE_FRACTION
    inv_freq = 1.0 / (ROPE_THETA ** (jnp.arange(0, rot, 2, dtype=F32) / rot))
    ang = positions.astype(F32)[..., None] * inv_freq
    return jnp.cos(ang)[:, :, None, :], jnp.sin(ang)[:, :, None, :]

def rope_partial(t, cos, sin):
    half = cos.shape[-1]
    t1 = t[..., :half]
    t2 = t[..., half:2 * half]
    out = jnp.concatenate([t1 * cos - t2 * sin, t2 * cos + t1 * sin, t[..., 2 * half:]], axis=-1)
    return out.astype(t.dtype)

def dsa_attention(q, k, v, iq, ik, iw):
    B, S, H, Dh = q.shape
    n_sel = min(TOPK_MAX, S // 4)
    nb = S // Q_BLOCK
    idx_scale = (IDX_HEADS ** -0.5) * (IDX_HD ** -0.5)
    key_pos = jnp.arange(S)
    ikf = ik.astype(F32)

    def blocks(t):
        return jnp.moveaxis(t.reshape(B, nb, Q_BLOCK, *t.shape[2:]), 1, 0)

    def one_block(args):
        qb, iqb, iwb, tq = args
        logits = jnp.einsum('bqhd,bsd->bqhs', iqb.astype(F32), ikf)
        score = jnp.einsum('bqh,bqhs->bqs', iwb.astype(F32) * idx_scale, jax.nn.relu(logits))
        causal = key_pos[None, None, :] <= tq[None, :, None]
        score = jnp.where(causal, score, -jnp.inf)
        _, sel = lax.top_k(score, n_sel)
        valid = sel <= tq[None, :, None]
        k_sel = jax.vmap(lambda kk, ii: kk[ii])(k, sel)
        v_sel = jax.vmap(lambda vv, ii: vv[ii])(v, sel)
        att = jnp.einsum('bqhd,bqnhd->bhqn', qb.astype(F32), k_sel.astype(F32)) * (Dh ** -0.5)
        att = jnp.where(valid[:, None], att, -jnp.inf)
        p = jax.nn.softmax(att, axis=-1)
        out = jnp.einsum('bhqn,bqnhd->bqhd', p, v_sel.astype(F32))
        return out.astype(q.dtype)

    tq_blocks = jnp.arange(S).reshape(nb, Q_BLOCK)
    out = lax.map(one_block, (blocks(q), blocks(iq), blocks(iw), tq_blocks))
    return jnp.moveaxis(out, 0, 1).reshape(B, S, H * Dh)

def wkv7_scan(r, w, k, v, a, b):
    B, S, H, N = r.shape
    tm = lambda t: jnp.moveaxis(t, 1, 0)

    def step(state, inp):
        r_t, w_t, k_t, v_t, a_t, b_t = inp
        sa = jnp.einsum('bhij,bhj->bhi', state, a_t)
        state = state * w_t[:, :, None, :] + sa[..., None] * b_t[:, :, None, :] + v_t[..., :, None] * k_t[:, :, None, :]
        y = jnp.einsum('bhij,bhj->bhi', state, r_t)
        return state, y

    state0 = jnp.zeros((B, H, N, N), F32)
    _, ys = lax.scan(step, state0, (tm(r), tm(w), tm(k), tm(v), tm(a), tm(b)))
    return jnp.moveaxis(ys, 0, 1)

def rwkv7_time_mix(p, mu, w0, w2, a0, a2, g2, k_k, k_a, r_k, ln_w, ln_b):
    B, S, _ = p.shape
    prev = jnp.pad(p, ((0, 0), (1, 0), (0, 0)))[:, :-1]
    p = p + (prev - p) * mu
    r, k, v, wd, ad, gd = [t.astype(F32) for t in split_last(p, (RWKV_W, RWKV_W, RWKV_W, DECAY_LORA, AAA_LORA, GATE_LORA))]
    w_log = -jax.nn.softplus(-(w0.astype(F32) + jnp.tanh(wd) @ w2.astype(F32))) - 0.5
    decay = jnp.exp(-jnp.exp(w_log))
    a = jax.nn.sigmoid(a0.astype(F32) + ad @ a2.astype(F32))
    g = jax.nn.sigmoid(gd) @ g2.astype(F32)
    heads = lambda t: t.reshape(B, S, RWKV_HEADS, RWKV_HD)
    kk = heads(k * k_k.astype(F32))
    kk = kk / jnp.maximum(jnp.sqrt(jnp.sum(kk * kk, axis=-1, keepdims=True)), 1e-12)
    k = k * (1.0 + (a - 1.0) * k_a.astype(F32))
    rh, kh, vh, wh, ah = heads(r), heads(k), heads(v), heads(decay), heads(a)
    y = wkv7_scan(rh, wh, kh, vh, -kk, kk * ah)
    mean = jnp.mean(y, axis=-1, keepdims=True)
    var = jnp.mean(jnp.square(y - mean), axis=-1, keepdims=True)
    y = (y - mean) * lax.rsqrt(var + GN_EPS) * ln_w.astype(F32).reshape(RWKV_HEADS, RWKV_HD) + ln_b.astype(F32).reshape(RWKV_HEADS, RWKV_HD)
    y = y + jnp.sum(rh * kh * r_k.astype(F32), axis=-1, keepdims=True) * vh
    return (y.reshape(B, S, RWKV_W) * g).astype(p.dtype)

def memory_cross_attention(q_p, mem, mem_norm_gain, w_mem_kv, q_gain, k_gain):
    B, S, _ = q_p.shape
    M = mem.shape[1]
    m = rmsnorm(mem, mem_norm_gain)
    km, vm = split_last(m @ w_mem_kv, (MEM_W, MEM_W))
    q = rmsnorm(q_p.reshape(B, S, MEM_HEADS, MEM_HD), q_gain)
    km = rmsnorm(km.reshape(B, M, MEM_HEADS, MEM_HD), k_gain)
    vm = vm.reshape(B, M, MEM_HEADS, MEM_HD)
    s = jnp.einsum('bqhd,bmhd->bhqm', q.astype(F32), km.astype(F32)) * (MEM_HD ** -0.5)
    p = jax.nn.softmax(s, axis=-1)
    out = jnp.einsum('bhqm,bmhd->bqhd', p, vm.astype(F32))
    return out.reshape(B, S, MEM_W).astype(q_p.dtype)

def peer_ffn(xn, w_q, key1, key2, u, v):
    B, S, D = xn.shape
    q = (xn @ w_q).reshape(B, S, PEER_HEADS, 2, PEER_QDIM // 2).astype(F32)
    s1 = jnp.einsum('bshd,kd->bshk', q[..., 0, :], key1.astype(F32))
    s2 = jnp.einsum('bshd,kd->bshk', q[..., 1, :], key2.astype(F32))
    v1, i1 = lax.top_k(s1, PEER_TOPK)
    v2, i2 = lax.top_k(s2, PEER_TOPK)
    cand = (v1[..., :, None] + v2[..., None, :]).reshape(B, S, PEER_HEADS, PEER_TOPK * PEER_TOPK)
    sc, ci = lax.top_k(cand, PEER_TOPK)
    e1 = jnp.take_along_axis(i1, ci // PEER_TOPK, axis=-1)
    e2 = jnp.take_along_axis(i2, ci % PEER_TOPK, axis=-1)
    expert = e1 * PEER_KEYS + e2
    gate = jax.nn.softmax(sc, axis=-1)
    T = B * S
    E = PEER_HEADS * PEER_TOPK
    nb = T // PEER_BLOCK
    xb = xn.reshape(nb, PEER_BLOCK, D)
    eb = expert.reshape(nb, PEER_BLOCK, E)
    gb = gate.reshape(nb, PEER_BLOCK, E)

    def one_block(args):
        xt, et, gt = args
        ue = u[et].astype(F32)
        ve = v[et].astype(F32)
        hid = jax.nn.gelu(jnp.einsum('td,ted->te', xt.astype(F32), ue), approximate=False)
        return jnp.einsum('te,ted->td', gt * hid, ve).astype(xt.dtype)

    out = lax.map(one_block, (xb, eb, gb))
    return out.reshape(B, S, D)

def hybrid_layer(h, mem, cos, sin, mix_norm_gain, w_in, gate_bias, att_q_gain, att_k_gain, mem_norm_gain, w_mem_kv, mem_q_gain, mem_k_gain, rwkv_mu, rwkv_w0, rwkv_w2, rwkv_a0, rwkv_a2, rwkv_g2, rwkv_k_k, rwkv_k_a, rwkv_r_k, rwkv_ln_w, rwkv_ln_b, w_up, w_out, ffn_norm_gain, peer_w_q, peer_key1, peer_key2, peer_u, peer_v):
    B, S, D = h.shape
    n = rmsnorm(h, mix_norm_gain)
    proj = n @ w_in
    att_p, rwkv_p, memq_p, gate_p = split_last(proj, (ATT_IN, RWKV_IN, MEM_W, GATE_IN))
    q, k, v, iq, ik, iw = split_last(att_p, (ATT_W, ATT_W, ATT_W, IDX_HEADS * IDX_HD, IDX_HD, IDX_HEADS))
    q = rope_partial(rmsnorm(q.reshape(B, S, ATT_HEADS, ATT_HD), att_q_gain), cos, sin)
    k = rope_partial(rmsnorm(k.reshape(B, S, ATT_HEADS, ATT_HD), att_k_gain), cos, sin)
    v = v.reshape(B, S, ATT_HEADS, ATT_HD)
    iq = rope_partial(iq.reshape(B, S, IDX_HEADS, IDX_HD), cos, sin)
    ik = rope_partial(ik[:, :, None, :], cos, sin)[:, :, 0]
    y_att = dsa_attention(q, k, v, iq, ik, iw)
    y_rwkv = rwkv7_time_mix(rwkv_p, rwkv_mu, rwkv_w0, rwkv_w2, rwkv_a0, rwkv_a2, rwkv_g2, rwkv_k_k, rwkv_k_a, rwkv_r_k, rwkv_ln_w, rwkv_ln_b)
    y_mem = memory_cross_attention(memq_p, mem, mem_norm_gain, w_mem_kv, mem_q_gain, mem_k_gain)
    branches = jnp.stack([y_att.astype(F32), y_rwkv.astype(F32), y_mem.astype(F32)], axis=2)
    up = jnp.einsum('bscw,cwd->bscd', branches, w_up.astype(F32))
    gates = jax.nn.sigmoid(gate_p.reshape(B, S, N_BRANCH, D).astype(F32) + gate_bias.astype(F32))
    merged = jnp.sum(gates * up, axis=2).astype(h.dtype)
    h = h + merged @ w_out
    h = h + peer_ffn(rmsnorm(h, ffn_norm_gain), peer_w_q, peer_key1, peer_key2, peer_u, peer_v)
    return h

def setup_inputs(seed: int = 0) -> dict:
    key = jax.random.key(seed)
    ks = iter(jax.random.split(key, 48))
    L = DEPTH

    def nrm(shape, scale):
        return jax.random.normal(next(ks), shape, F32) * scale

    def gain(shape):
        return 1.0 + nrm(shape, 0.05)

    x = nrm((BATCH, SEQ, D_MODEL), 1.0)
    mem = nrm((BATCH, N_MEM, D_MODEL), 1.0)
    positions = jax.random.randint(next(ks), (BATCH, 1), 0, 4096, dtype=jnp.int32) + jnp.arange(SEQ, dtype=jnp.int32)[None, :]
    return {
        'x': x,
        'mem': mem,
        'positions': positions,
        'mix_norm_gain': gain((L, D_MODEL)),
        'w_in': nrm((L, D_MODEL, W_IN_COLS), D_MODEL ** -0.5),
        'gate_bias': nrm((L, N_BRANCH, D_MODEL), 0.1),
        'att_q_gain': gain((L, ATT_HD)),
        'att_k_gain': gain((L, ATT_HD)),
        'mem_norm_gain': gain((L, D_MODEL)),
        'w_mem_kv': nrm((L, D_MODEL, 2 * MEM_W), D_MODEL ** -0.5),
        'mem_q_gain': gain((L, MEM_HD)),
        'mem_k_gain': gain((L, MEM_HD)),
        'rwkv_mu': jax.random.uniform(next(ks), (L, RWKV_IN), F32, 0.0, 1.0),
        'rwkv_w0': jax.random.uniform(next(ks), (L, RWKV_W), F32, -3.0, 0.0),
        'rwkv_w2': nrm((L, DECAY_LORA, RWKV_W), 0.5 * DECAY_LORA ** -0.5),
        'rwkv_a0': nrm((L, RWKV_W), 0.1),
        'rwkv_a2': nrm((L, AAA_LORA, RWKV_W), 0.5 * AAA_LORA ** -0.5),
        'rwkv_g2': nrm((L, GATE_LORA, RWKV_W), GATE_LORA ** -0.5),
        'rwkv_k_k': 0.85 + nrm((L, RWKV_W), 0.05),
        'rwkv_k_a': gain((L, RWKV_W)),
        'rwkv_r_k': nrm((L, RWKV_HEADS, RWKV_HD), 0.1),
        'rwkv_ln_w': gain((L, RWKV_W)),
        'rwkv_ln_b': nrm((L, RWKV_W), 0.02),
        'w_up': nrm((L, N_BRANCH, BRANCH_W, D_MODEL), BRANCH_W ** -0.5),
        'w_out': nrm((L, D_MODEL, D_MODEL), D_MODEL ** -0.5),
        'ffn_norm_gain': gain((L, D_MODEL)),
        'peer_w_q': nrm((L, D_MODEL, PEER_HEADS * PEER_QDIM), D_MODEL ** -0.5),
        'peer_key1': nrm((L, PEER_KEYS, PEER_QDIM // 2), (PEER_QDIM // 2) ** -0.5),
        'peer_key2': nrm((L, PEER_KEYS, PEER_QDIM // 2), (PEER_QDIM // 2) ** -0.5),
        'peer_u': nrm((L, N_EXPERTS, D_MODEL), D_MODEL ** -0.5),
        'peer_v': nrm((L, N_EXPERTS, D_MODEL), PEER_HEADS ** -0.5),
    }

def reference(x, mem, positions, mix_norm_gain, w_in, gate_bias, att_q_gain, att_k_gain, mem_norm_gain, w_mem_kv, mem_q_gain, mem_k_gain, rwkv_mu, rwkv_w0, rwkv_w2, rwkv_a0, rwkv_a2, rwkv_g2, rwkv_k_k, rwkv_k_a, rwkv_r_k, rwkv_ln_w, rwkv_ln_b, w_up, w_out, ffn_norm_gain, peer_w_q, peer_key1, peer_key2, peer_u, peer_v):
    cos, sin = rope_tables(positions, ATT_HD)
    h = x
    for layer in range(DEPTH):
        h = hybrid_layer(h, mem, cos, sin, mix_norm_gain[layer], w_in[layer], gate_bias[layer], att_q_gain[layer], att_k_gain[layer], mem_norm_gain[layer], w_mem_kv[layer], mem_q_gain[layer], mem_k_gain[layer], rwkv_mu[layer], rwkv_w0[layer], rwkv_w2[layer], rwkv_a0[layer], rwkv_a2[layer], rwkv_g2[layer], rwkv_k_k[layer], rwkv_k_a[layer], rwkv_r_k[layer], rwkv_ln_w[layer], rwkv_ln_b[layer], w_up[layer], w_out[layer], ffn_norm_gain[layer], peer_w_q[layer], peer_key1[layer], peer_key2[layer], peer_u[layer], peer_v[layer])
    return h


_drawn_inputs = setup_inputs


def setup_inputs(seed=0):
    import zlib

    import numpy as np

    out = dict(_drawn_inputs(seed))
    spreads = {}
    factors = {'att_q_gain': 3.762,
     'att_k_gain': 4.12,
     'mem_norm_gain': 4.507,
     'mem_q_gain': 5.355,
     'mem_k_gain': 5.645,
     'rwkv_k_k': 33.336,
     'rwkv_ln_b': 19.929,
     'rwkv_w2': 6.741,
     'rwkv_a0': 7.568,
     'rwkv_k_a': 6.927,
     'rwkv_ln_w': 7.496,
     'ffn_norm_gain': 3.446}
    for name, (base, spread) in spreads.items():
        noise = np.random.default_rng([zlib.crc32(name.encode()), seed]).standard_normal(out[name].shape)
        drawn = base * np.exp(spread * noise) if base else spread * noise
        out[name] = __import__('jax').numpy.asarray(drawn.astype(out[name].dtype))
    for name, factor in factors.items():
        out[name] = (out[name] * factor).astype(out[name].dtype)
    return out
```

```python
from contextlib import ExitStack

import numpy as np
import concourse.bass as bass
from concourse import mybir

P = 128
D = 1024
S = 256
TILES = S // P
KT = D // P
W = 512
CT = W // P
HD = 64
HEADS = W // HD
CHUNK = 64
NCHUNK = S // CHUNK
MEM_HEADS = 4
IDX_HEADS = 4
N_SEL = 64
LEVELS = 6
PEER_HEADS = 8
TOPK = 16
KEYS = 128
EPS = 1e-6
GN_EPS = 64e-5
DECAY = float(np.exp(-0.5))
OFF = -1.0e30
TAKEN = -3.0e38
BLOCK = 2048
RING = 3
POOL_COLS = 187 * 256
SLOTS = 16
GROUP = 4

F32 = mybir.dt.float32
I32 = mybir.dt.int32
U32 = mybir.dt.uint32
ALU = mybir.AluOpType
ACT = mybir.ActivationFunctionType
AX = mybir.AxisListType.X

STREAM = [("rwkv", 7), ("mem_k", 2), ("mem_v", 2), ("mem_q", 2), ("idx_q", 1), ("idx_k", 1),
          ("q", 2), ("k", 2), ("v", 2), ("gate", 12), ("up", 6), ("out", 4), ("peer_q", 8)]
BLOCKS = sum(n for _, n in STREAM)
FIRST_BLOCK = {}
FIRST_UNIT = {}
_b = _u = 0
for _name, _n in STREAM:
    FIRST_BLOCK[_name], FIRST_UNIT[_name] = _b, _u
    _b += _n
    _u += _n * (2 if _name == "up" else 1)

CONST = {}
_c = 0
for _name, _n in [("ident", 128), ("head_ones", 128), ("ones", 128), ("rot", 128), ("causal", 128),
                  ("gram_mask", 512), ("level", 128 * LEVELS), ("headsel", 2), ("iota", 16), ("inv_freq", 1)]:
    CONST[_name] = (_c, _n)
    _c += _n
CONST_COLS = _c

VEC = {}
_c = 0
for _name, _n in [("mix_gain", 8), ("mem_gain", 8), ("gate_bias", 24), ("mu", 14), ("w0", 4), ("a0", 4),
                  ("k_k", 4), ("k_a", 4), ("r_k", 4), ("q_gain", 1), ("k_gain", 1), ("mq_gain", 1), ("mk_gain", 1)]:
    VEC[_name] = (_c, _n)
    _c += _n
VEC_COLS = _c


def constants():
    p = np.arange(P)
    out = {}
    out["ident"] = np.eye(P)
    out["head_ones"] = (p[:, None] // HD == p[None, :] // HD).astype(np.float64)
    out["ones"] = np.ones((P, P))
    rot = np.zeros((P, P))
    for base in (0, HD):
        for i in range(8):
            rot[base + 8 + i, base + i] = -1.0
            rot[base + i, base + 8 + i] = 1.0
    out["rot"] = rot
    out["causal"] = np.where(p[None, :] <= p[:, None], 0.0, OFF)
    s, t = p[:, None], p[None, :]
    same = s // CHUNK == t // CHUNK
    strict, incl = same & (s < t), same & (s <= t)
    out["gram_mask"] = np.concatenate([strict, incl, strict, incl], axis=1)
    out["level"] = np.concatenate(
        [(s // (2 << l) == t // (2 << l)) & ((t >> l) % 2 == 1) & ((s >> l) % 2 == 0) for l in range(LEVELS)], axis=1)
    out["headsel"] = (p[:, None] // HD == np.arange(2)[None, :])
    out["iota"] = np.tile(np.arange(16), (P, 1))
    inv = (np.float32(1.0) / (np.float32(500000.0) ** (np.arange(0, 16, 2, dtype=np.float32) / np.float32(16))))
    col = np.zeros(P)
    for q in range(P):
        if q % HD < 16:
            col[q] = inv[(q % HD) % 8]
    out["inv_freq"] = col[:, None]
    return np.ascontiguousarray(np.concatenate([out[n] for n in CONST], axis=1).astype(np.float32))


def job_plan():
    jobs = []
    for src in ("x", "mem"):
        jobs += [(src, t, q) for t in range(TILES) for q in range(2)]
    jobs += [("wl", i) for i in range(2)] + [("al", i) for i in range(2)]
    jobs += [("kn", i) for i in range(2)]
    jobs += [("vt", t) for t in range(TILES)]
    jobs += [("mk_ss", i) for i in range(2)] + [("mq_ss", i) for i in range(2)]
    jobs += [("bt", 0), ("bt", 1), ("kt", 0), ("kt", 1), ("bonus", 0), ("bonus", 1)]
    jobs += [("ms", t, hp) for t in range(TILES) for hp in range(2)]
    jobs += [("iqrot", 0), ("ikrot", 0)]
    jobs += [("il", t, i) for t in range(TILES) for i in range(2)]
    jobs += [(f"mpt", t, hp) for t in range(TILES) for hp in range(2)]
    jobs += [("mpv", hp) for hp in range(2)]
    for x in ("q", "k"):
        jobs += [(x + "_ss", i) for i in range(2)]
    for x in ("q", "k"):
        jobs += [(x + "rot", i) for i in range(2)]
    jobs += [("as", hp, m) for hp in range(2) for m in range(2)]
    for hp in range(4):
        jobs += [("apt", hp, i) for i in range(2)]
        jobs += [("apv", hp)]
        if hp < 2:
            jobs += [("as", hp + 2, m) for m in range(2)]
    for t in range(TILES):
        if t == 0:
            jobs += [("g", 0), ("g", 1)]
        jobs += [("gram", t, h) for h in range(HEADS)]
        for l in range(LEVELS):
            jobs += [("A", t, l, g) for g in range(2)]
            if 0 < l < LEVELS - 1:
                jobs += [("X", t, l, g) for g in range(2)]
            if l > 0:
                jobs += [("XT", t, l, g) for g in range(2)]
        for n in (2 * t, 2 * t + 1):
            jobs += [("rhs", n), ("U", n), ("Y", n)]
            if n < NCHUNK - 1:
                jobs += [("S", n)]
        jobs += [("yt", t)]
    jobs += [("xn", t, q) for t in range(TILES) for q in range(2)]
    for h in range(PEER_HEADS):
        jobs += [("ps", h)]
    return {j: n for n, j in enumerate(jobs)}


JOB = job_plan()
BANKS = 6


def build(nc, t_in, out):
    ctx = ExitStack()
    with ctx:
        def sb(name, shape, dt=F32):
            return ctx.enter_context(nc.sbuf_tensor(name, shape, dt))

        def sem(name):
            return ctx.enter_context(nc.semaphore(name))

        const = sb("const", [P, CONST_COLS])
        vec = sb("vec", [P, VEC_COLS])
        trig = sb("trig", [P, 2, S])
        lora = sb("lora", [P, W])
        glora = sb("glora", [P, W])
        rows = sb("rows", [P, 2 * W])
        small = sb("small", [P, 160])
        pos_i = sb("pos_i", [P, S], I32)
        pool_mem = sb("pool_mem", [P, POOL_COLS])

        def part(at, *shape):
            n = int(np.prod(shape))
            assert at + n <= POOL_COLS, (at, n)
            v = pool_mem[:, at:at + n]
            if len(shape) == 2:
                return v.rearrange("p (a b) -> p a b", a=shape[0])
            if len(shape) == 3:
                return v.rearrange("p (a b c) -> p a b c", a=shape[0], b=shape[1])
            if len(shape) == 4:
                return v.rearrange("p (a b c d) -> p a b c d", a=shape[0], b=shape[1], c=shape[2])
            return v

        K1 = 256
        G = 0
        gates = part(G, 24, S)
        rope_raw = {"q": part(G, CT, S), "k": part(G + 12 * K1, CT, S)}
        rope_sq = {"q": part(G + 4 * K1, CT, S), "k": part(G + 16 * K1, CT, S)}
        rope_rn = {"q": part(G + 8 * K1, CT, S), "k": part(G + 20 * K1, CT, S)}
        h_tok = part(G, TILES, D)
        xn_tok = part(G + 8 * K1, TILES, D)
        N0 = G + 24 * K1
        nT = part(N0, KT, S)
        scores = part(G + 16 * K1, (PEER_HEADS * TILES + 2) * 256)
        E0 = N0 + 8 * K1
        iqT = part(E0, 2, S)
        ikT = part(E0 + 2 * K1, S)
        score = part(E0 + 3 * K1, TILES, S)
        work = part(E0 + 5 * K1, TILES, S)
        Y0 = E0 + 7 * K1
        y_att = part(Y0, CT, S)
        y_mem = part(Y0 + 4 * K1, CT, S)
        R0 = Y0 + 8 * K1
        wring = [part(R0 + BLOCK * i, KT, 256) for i in range(RING)]
        T0 = R0 + RING * BLOCK
        mT = part(T0, KT, S)
        kmT = part(T0 + 8 * K1, CT, S)
        vm = part(T0 + 12 * K1, TILES, W)
        mqT = part(T0 + 16 * K1, CT, S)
        mem_sq = {"mk": part(T0 + 20 * K1, CT, S), "mq": part(T0 + 28 * K1, CT, S)}
        mem_rn = {"mk": part(T0 + 24 * K1, CT, S), "mq": part(T0 + 32 * K1, CT, S)}
        mprob = part(T0 + 20 * K1, TILES, MEM_HEADS, S)
        mprobT = part(T0 + 28 * K1, TILES, MEM_HEADS, TILES, P)
        qT = part(T0, CT, S)
        kT = part(T0 + 4 * K1, CT, S)
        v_tok = part(T0 + 8 * K1, TILES, W)
        bias = part(T0 + 16 * K1, TILES, S)
        prob = part(T0 + 20 * K1, 4, 2, S)
        probT = part(T0 + 28 * K1, 4, 2, 2, P)
        merged = part(T0, KT, S)
        xnT = part(T0 + 8 * K1, KT, S)
        tmp_up = part(T0 + 16 * K1, 2, S)
        idx_relu = part(T0 + 36 * K1 + 54 * K1, 2, S)
        Q0 = T0 + 36 * K1
        x_tok = {"x": part(Q0, TILES, D), "mem": part(Q0 + 8 * K1, TILES, D)}
        x_scaled = {"x": part(Q0 + 16 * K1, TILES, D), "mem": part(Q0 + 24 * K1, TILES, D)}
        ar = part(Q0, CT, 2, S)
        bb = part(Q0 + 8 * K1, CT, S)
        kb = part(Q0 + 12 * K1, CT, S)
        vtok = part(Q0 + 16 * K1, TILES, W)
        btok = part(Q0 + 20 * K1, TILES, W)
        ktok = part(Q0 + 24 * K1, TILES, W)
        kmod = part(Q0 + 28 * K1, CT, S)
        gtok = part(Q0 + 28 * K1, TILES, W)
        knorm = part(Q0 + 32 * K1, CT, S)
        ytok = part(Q0 + 32 * K1, TILES, W)
        mixed = part(Q0 + 36 * K1, 14, S)
        pT = part(Q0 + 50 * K1, 14, S + 1)
        sgw = part(Q0 + 50 * K1, CT, S)
        a_gate = part(Q0 + 54 * K1, CT, S)
        cum = part(Q0 + 58 * K1, CT, S)
        b_end = part(Q0 + 62 * K1, CT, S)
        k_end = part(Q0 + 50 * K1, CT, S)
        p_inv = part(Q0 + 68 * K1, CT, S)
        rkk = part(Q0 + 68 * K1, CT, S)
        p_ex = part(Q0 + 72 * K1, CT, S)
        kk = part(Q0 + 76 * K1, CT, S)
        gram = part(Q0 + 36 * K1, HEADS, 4, P)
        X = part(Q0 + 52 * K1, HEADS, P)
        XT = part(Q0 + 56 * K1, HEADS, P)
        A1 = part(Q0 + 60 * K1, HEADS, P)
        LmT = part(Q0 + 64 * K1, HEADS, P)
        y_rwkv = part(Q0 + 68 * K1, CT, S)
        state = part(Q0 + 72 * K1, CT, P)
        rhs_sb = part(Q0 + 74 * K1, W)
        U = part(Q0 + 76 * K1, W)
        gn_tmp = part(Q0 + 78 * K1, W)
        x_again = part(Q0, TILES, D)
        gain_row = part(Q0 + 8 * K1, D)
        qp = [part(Q0 + 12 * K1 + 512 * i, 2, S) for i in range(2)]
        keysT = part(Q0 + 16 * K1, 2, KEYS)
        RING0 = G + 34 * K1
        slot = [part(RING0 + BLOCK * i, BLOCK) for i in range(SLOTS)]
        o_sb = part(RING0 + BLOCK * SLOTS, D)

        at = [RING0 + BLOCK * SLOTS + D]

        def tail(dt, *shape):
            n = int(np.prod(shape))
            a = part(at[0], *shape) if dt == F32 else None
            if a is None:
                a = pool_mem[:, at[0]:at[0] + n].bitcast(dt)
                if len(shape) == 2:
                    a = a.rearrange("p (a b) -> p a b", a=shape[0])
            at[0] += n
            assert at[0] <= POOL_COLS
            return a

        stage = tail(F32, 2, 2, KEYS)
        best = tail(F32, 2, TOPK)
        best_i = tail(U32, 2, TOPK)
        best_f = tail(F32, 2, TOPK)
        cand = tail(F32, TOPK, TOPK)
        top = tail(F32, 2, TOPK)
        top_i = tail(U32, TOPK)
        place_i = tail(U32, 2, TOPK)
        place_f = tail(F32, 2, TOPK)
        onehot = tail(F32, 2 * TOPK, TOPK)
        expert = tail(F32, 2, TOPK)
        expert_f = tail(F32, TOPK)
        expert_i = tail(U32, 2, TOPK)
        gate_e = tail(F32, 2, TOPK)
        gstat = tail(F32, 2, 4)
        hid = tail(F32, 2, TOPK)
        act_h = tail(F32, 2, TOPK)
        diag = tail(F32, 2 * GROUP, P)

        psum_proj = ctx.enter_context(nc.psum_tensor("psum_proj", [P, 2, 512], F32))
        psum_job = ctx.enter_context(nc.psum_tensor("psum_job", [P, BANKS, 512], F32))

        def c(name):
            a, n = CONST[name]
            return const[:, a:a + n]

        def v(name, i=0, n=1):
            a, _ = VEC[name]
            return vec[:, a + i:a + i + n]

        ident = c("ident")

        def sm(i, n=1):
            return small[:, i:i + n]
        SSQ, ROOT, RSTD = 0, 4, 8
        OMKA = 12
        IW = 16
        BON = 24
        MX = 40
        SU = 56
        RS = 72
        GN = 88
        HS = 112
        NMX = 120
        EPSC = 118
        eps_col, gn_eps_col = sm(EPSC), sm(EPSC + 1)
        pend = sm(128, CT * NCHUNK)
        w_tanh = part(Q0 + 66 * K1, S)[0:64]
        g_sig = part(Q0 + 67 * K1, S)
        reset = part(E0 + 2 * K1, S)

        consts_in, params_in = sem("consts_in"), sem("params_in")
        tokens_in = {"x": sem("x_in"), "mem": sem("mem_in")}
        late_in = sem("late_in")
        weights_in = [sem(f"weights_in{i}") for i in range(RING)]
        proj_full = sem("proj_full")
        proj_free = [sem(f"proj_free{i}") for i in range(2)]
        bank_full = [sem(f"bank_full{i}") for i in range(BANKS)]
        bank_free = [sem(f"bank_free{i}") for i in range(BANKS)]
        dve_step, act_step, pool_step = sem("dve_step"), sem("act_step"), sem("pool_step")
        names = ["ssq", "root", "scaled", "mixed_ok", "lora_in", "sg_ok", "kk_ok", "kk2_ok", "cum_ok", "lex_ok",
                 "decay_ok", "kn_ok", "kroot", "ends_ok", "a_ok", "tilde_ok", "msq_ok", "mroot", "mnorm_ok",
                 "mexp", "mscaled", "mmax", "trig_arg", "trig_ok", "iq_ok", "relu_ok", "relu_used", "sq_ok", "rroot",
                 "rn_ok", "rope_ok", "amax", "aexp", "ascaled", "lm_ok", "xt0", "pads", "u_ready", "s_ready",
                 "y_ready", "gn_sq", "gn_root", "yr_ready", "prod", "merged_ok", "h_ssq", "h_root", "xn_ok",
                 "stage_ok", "experts_ok", "gate_in", "gate_ok", "dots", "gelu_ok", "diag_ok", "group_free",
                 "o_start", "o_full", "o_sb_ok", "stored", "mix_pad", "stage_used", "scores_ok", "h_done", "gsum", "choose"]
        sg = {n: sem("s_" + n) for n in names}
        carried = {nc.vector.engine: sem("carried_dve"), nc.gpsimd.engine: sem("carried_pool")}
        slot_in = [sem(f"slot_in{i}") for i in range(SLOTS)]

        class Steps:
            def __init__(self, eng, s):
                self.eng, self.s, self.n = eng, s, 0

            def __call__(self, ins):
                ins.then_inc(self.s, 1)
                self.n += 1
                return self

            def wait(self):
                self.eng.wait_ge(self.s, self.n)

        def bank(job):
            return psum_job[:, JOB[job] % BANKS, :]

        def wait_job(eng, job):
            eng.wait_ge(bank_full[JOB[job] % BANKS], JOB[job] // BANKS + 1)

        def job_read(ins, job):
            return ins.then_inc(bank_free[JOB[job] % BANKS], 1)

        def wait_read(eng, job):
            eng.wait_ge(bank_free[JOB[job] % BANKS], JOB[job] // BANKS + 1)

        def unit(name, i):
            return FIRST_UNIT[name] + i

        def ubank(name, i):
            return psum_proj[:, unit(name, i) % 2, :]

        def wait_unit(eng, name, i):
            eng.wait_ge(proj_full, unit(name, i) + 1)

        def unit_read(ins, name, i):
            return ins.then_inc(proj_free[unit(name, i) % 2], 1)

        def wait_unit_read(eng, name, i):
            eng.wait_ge(proj_free[unit(name, i) % 2], unit(name, i) // 2 + 1)

        def wait_alone(eng, s, value):
            eng.wait_ge(s, value)
            eng.sem_inc(carried[eng.engine], 1)

        def halves(ap):
            return ap.rearrange("p (a b) -> p a b", a=2)

        def key_scores(pe, mm, begin, end, h):
            wait_unit_read(pe, "peer_q", h)
            if h == 0:
                pe.wait_ge(late_in, 48)
            o = begin(("ps", h))
            for t in range(TILES):
                for m in range(2):
                    ins = mm(o[:, (2 * t + m) * KEYS:(2 * t + m + 1) * KEYS], lhsT=qp[h % 2][:, m, t * P:(t + 1) * P],
                             rhs=keysT[:, m, :], start=True, stop=True)
            end(ins, ("ps", h))

        def diagonals(dve, V, done, par, g):
            dve.wait_ge(sg["gelu_ok"], done)
            dve.wait_ge(sg["group_free"], done + 2)
            for s_ in range(GROUP * g, GROUP * g + GROUP):
                ins = V.tensor_scalar(diag[:, s_ % (2 * GROUP), :], ident, act_h[:, par, s_:s_ + 1],
                                      gate_e[:, par, s_:s_ + 1], ALU.mult, ALU.mult)
            ins.then_inc(sg["diag_ok"], 1)

        block = ctx.enter_context(nc.Block())

        @block.sync
        def _(sp):
            sp.dma_start(x_tok["x"], t_in["x"].rearrange("(t p) d -> p t d", p=P)).then_inc(tokens_in["x"], 16)
            sp.dma_start(const[:, :], t_in["const"]).then_inc(consts_in, 16)
            sp.dma_start(vec[:, :], t_in["vec"]).then_inc(params_in, 16)
            sp.dma_start(x_tok["mem"], t_in["mem"].rearrange("(t p) d -> p t d", p=P)).then_inc(tokens_in["mem"], 16)
            for b in range(RING):
                sp.dma_start(wring[b].rearrange("p a b -> p (a b)"), t_in["weights"][b]).then_inc(weights_in[b], 16)
            sp.dma_start(pos_i[:, :], t_in["positions"].partition_broadcast(P)).then_inc(params_in, 16)
            sp.dma_start(lora[:, :], t_in["lora"]).then_inc(params_in, 16)
            sp.dma_start(glora[:, :], t_in["glora"]).then_inc(params_in, 16)
            sp.dma_start(rows[:, :], t_in["rows"].partition_broadcast(P)).then_inc(params_in, 16)
            steady = FIRST_BLOCK["up"] // RING
            with sp.Fori(1, steady) as i:
                for b in range(RING):
                    sp.wait_ge(proj_full, i * RING + (b - RING + 1))
                    sp.dma_start(wring[b].rearrange("p a b -> p (a b)"),
                                 t_in["weights"][bass.ds(i * RING + b, 1)].rearrange("o p n -> (o p) n")
                                 ).then_inc(weights_in[b], 16)
            for b in range(steady * RING, BLOCKS):
                old = b - RING
                last = old + 1
                if old >= FIRST_BLOCK["up"]:
                    last = FIRST_UNIT["up"] + 2 * min(old - FIRST_BLOCK["up"] + 1, 6) \
                        + max(old - FIRST_BLOCK["out"] + 1, 0)
                sp.wait_ge(proj_full, last)
                sp.dma_start(wring[b % RING].rearrange("p a b -> p (a b)"),
                             t_in["weights"][b]).then_inc(weights_in[b % RING], 16)
                if b == FIRST_BLOCK["out"]:
                    sp.wait_ge(sg["y_ready"], 2)
                    sp.dma_start(x_again, t_in["x"].rearrange("(t p) d -> p t d", p=P)).then_inc(late_in, 16)
                    sp.dma_start(gain_row, t_in["ffn_gain"].partition_broadcast(P)).then_inc(late_in, 16)
                    sp.dma_start(keysT, t_in["keysT"]).then_inc(late_in, 16)
            for t in range(TILES):
                sp.wait_ge(sg["o_sb_ok"], 2 * t + 2)
                sp.dma_start(out[t * P:(t + 1) * P, :], o_sb).then_inc(sg["stored"], 16)
            sp.wait_ge(sg["stored"], 16 * TILES)

        @block.tensor
        def _(pe):
            mm, tr = nc.tensor.matmul, nc.tensor.transpose

            def begin(job):
                n = JOB[job]
                if n >= BANKS:
                    pe.wait_ge(bank_free[n % BANKS], n // BANKS)
                return psum_job[:, n % BANKS, :]

            def end(ins, job):
                ins.then_inc(bank_full[JOB[job] % BANKS], 1)

            def begin_unit(name, i, b=None):
                u = unit(name, i)
                blk = FIRST_BLOCK[name] + (i if b is None else b)
                pe.wait_ge(weights_in[blk % RING], 16 * (blk // RING + 1))
                if u >= 2:
                    pe.wait_ge(proj_free[u % 2], u // 2)
                return halves(psum_proj[:, u % 2, :]), wring[blk % RING]

            def channels(name, n, src):
                for i in range(n):
                    o, w = begin_unit(name, i)
                    for m in range(2):
                        for k in range(KT):
                            ins = mm(o[:, m, :], lhsT=w[:, k, m * P:(m + 1) * P], rhs=src[:, k, :],
                                     start=(k == 0), stop=(k == KT - 1))
                    ins.then_inc(proj_full, 1)

            def tokens(name, n, src, first=0):
                for i in range(first, n):
                    o, w = begin_unit(name, i)
                    for t in range(TILES):
                        for k in range(KT):
                            ins = mm(o[:, t, :], lhsT=src[:, k, t * P:(t + 1) * P], rhs=w[:, k, :],
                                     start=(k == 0), stop=(k == KT - 1))
                    ins.then_inc(proj_full, 1)

            def transposes(job, srcs):
                o = begin(job)
                for i, s in enumerate(srcs):
                    ins = tr(o[:, i * P:(i + 1) * P], s, ident)
                end(ins, job)

            pe.wait_ge(consts_in, 16)
            for src in ("x", "mem"):
                for t in range(TILES):
                    pe.wait_ge(sg["scaled"], (1 if src == "x" else 3) + t)
                    for q in range(2):
                        transposes((src, t, q), [x_scaled[src][:, t, (4 * q + i) * P:(4 * q + i + 1) * P] for i in range(4)])
            wait_read(pe, ("x", 1, 1))
            wait_read(pe, ("x", 1, 0))
            channels("rwkv", 7, nT)
            wait_read(pe, ("mem", 1, 1))
            wait_read(pe, ("mem", 1, 0))
            channels("mem_k", 2, mT)
            pe.wait_ge(params_in, 16 * 5)
            pe.wait_ge(sg["lora_in"], 1)
            for j, r0, src in (("wl", 0, w_tanh), ("al", 64, mixed[64:128, 12, :])):
                for i in range(2):
                    o = halves(begin((j, i)))
                    for m in range(2):
                        cc = 2 * i + m
                        ins = mm(o[:, m, :], lhsT=lora[r0:r0 + 64, cc * P:(cc + 1) * P], rhs=src, start=True, stop=True)
                    end(ins, (j, i))
            tokens("mem_v", 2, mT)
            pe.wait_ge(sg["kk2_ok"], 1)
            for i in range(2):
                o = begin(("kn", i))
                end(mm(o, lhsT=c("head_ones"), rhs=knorm[:, 2 * i:2 * i + 2, :].rearrange("p a b -> p (a b)"),
                       start=True, stop=True), ("kn", i))
            for t in range(TILES):
                transposes(("vt", t), [mixed[:, 8 + i, t * P:(t + 1) * P] for i in range(CT)])
            channels("mem_q", 2, nT)
            for x in ("mk", "mq"):
                for i in range(2):
                    wait_unit_read(pe, "mem_" + x[1], i)
                for i in range(2):
                    o = begin((x + "_ss", i))
                    end(mm(o, lhsT=c("ones"), rhs=mem_sq[x][:, 2 * i:2 * i + 2, :].rearrange("p a b -> p (a b)"),
                           start=True, stop=True), (x + "_ss", i))
            channels("idx_q", 1, nT)
            o, w = begin_unit("idx_k", 0)
            for k in range(KT):
                mm(o[:, 0, :], lhsT=w[:, k, 0:P], rhs=nT[:, k, :], start=(k == 0), stop=(k == KT - 1))
            for t in range(TILES):
                for k in range(KT):
                    ins = mm(o[:, 1, 4 * t:4 * t + 4], lhsT=nT[:, k, t * P:(t + 1) * P], rhs=w[:, k, P:P + 4],
                             start=(k == 0), stop=(k == KT - 1))
            ins.then_inc(proj_full, 1)
            channels("q", 2, nT)
            pe.wait_ge(sg["ends_ok"], 3)
            for j, src in (("bt", b_end), ("kt", k_end)):
                for t in range(TILES):
                    transposes((j, t), [src[:, i, t * P:(t + 1) * P] for i in range(CT)])
            for t in range(TILES):
                o = begin(("bonus", t))
                for i in range(CT):
                    ins = mm(o[:, 2 * i:2 * i + 2], lhsT=rkk[:, i, t * P:(t + 1) * P], rhs=c("headsel"),
                             start=True, stop=True)
                end(ins, ("bonus", t))
            pe.wait_ge(sg["mnorm_ok"], 2)
            for t in range(TILES):
                for hp in range(2):
                    o = halves(begin(("ms", t, hp)))
                    for m in range(2):
                        hh = 2 * hp + m
                        ins = mm(o[:, m, :], lhsT=mqT[:, hh, t * P:(t + 1) * P], rhs=kmT[:, hh, :], start=True, stop=True)
                    end(ins, ("ms", t, hp))
            channels("k", 2, nT)
            wait_unit_read(pe, "idx_q", 0)
            o = begin(("iqrot", 0))
            end(mm(o, lhsT=c("rot"), rhs=iqT.rearrange("p a b -> p (a b)"), start=True, stop=True), ("iqrot", 0))
            wait_unit_read(pe, "idx_k", 0)
            o = begin(("ikrot", 0))
            end(mm(o[:, 0:S], lhsT=c("rot"), rhs=ikT, start=True, stop=True), ("ikrot", 0))
            wait_read(pe, ("iqrot", 0))
            wait_read(pe, ("ikrot", 0))
            for t in range(TILES):
                for i in range(2):
                    o = halves(begin(("il", t, i)))
                    for m in range(2):
                        ins = mm(o[:, m, :], lhsT=iqT[64 * i:64 * i + 64, m, t * P:(t + 1) * P],
                                 rhs=ikT[64 * i:64 * i + 64, :], start=True, stop=True)
                    end(ins, ("il", t, i))
            tokens("v", 2, nT)
            for t in range(TILES):
                pe.wait_ge(sg["mscaled"], t + 1)
                for hp in range(2):
                    transposes(("mpt", t, hp), [mprob[:, t, 2 * hp + i // 2, (i % 2) * P:(i % 2 + 1) * P] for i in range(4)])
            for hp in range(2):
                o = halves(begin(("mpv", hp)))
                for t in range(TILES):
                    wait_read(pe, ("mpt", t, hp))
                for m in range(2):
                    hh = 2 * hp + m
                    for t in range(TILES):
                        for mt in range(TILES):
                            ins = mm(o[:, m, t * P:(t + 1) * P], lhsT=vm[:, mt, hh * P:(hh + 1) * P],
                                     rhs=mprobT[:, t, hh, mt, :], start=(mt == 0), stop=(mt == TILES - 1))
                end(ins, ("mpv", hp))
            for n, x in enumerate("qk"):
                wait_unit_read(pe, x, 0)
                wait_unit_read(pe, x, 1)
                for i in range(2):
                    o = begin((x + "_ss", i))
                    end(mm(o, lhsT=c("head_ones"), rhs=rope_sq[x][:, 2 * i:2 * i + 2, :].rearrange("p a b -> p (a b)"),
                           start=True, stop=True), (x + "_ss", i))
            for n, x in enumerate("qk"):
                pe.wait_ge(sg["rn_ok"], n + 1)
                for i in range(2):
                    o = begin((x + "rot", i))
                    end(mm(o, lhsT=c("rot"), rhs=rope_sq[x][:, 2 * i:2 * i + 2, :].rearrange("p a b -> p (a b)"),
                           start=True, stop=True), (x + "rot", i))
            pe.wait_ge(sg["rope_ok"], 2)
            def attention_scores(hp):
                for m in range(2):
                    o = halves(begin(("as", hp, m)))
                    for t in range(TILES):
                        ins = mm(o[:, t, :], lhsT=qT[64 * m:64 * m + 64, hp, t * P:(t + 1) * P],
                                 rhs=kT[64 * m:64 * m + 64, hp, :], start=True, stop=True)
                    end(ins, ("as", hp, m))

            attention_scores(0)
            attention_scores(1)
            for hp in range(4):
                pe.wait_ge(sg["ascaled"], hp + 1)
                for i in range(2):
                    transposes(("apt", hp, i), [prob[:, 2 * (hp % 2) + t, i, kt * P:(kt + 1) * P]
                                                for t in range(TILES) for kt in range(TILES)])
                o = halves(begin(("apv", hp)))
                wait_read(pe, ("apt", hp, 0))
                wait_read(pe, ("apt", hp, 1))
                if hp == 0:
                    wait_unit_read(pe, "v", 0)
                    wait_unit_read(pe, "v", 1)
                for m in range(2):
                    for t in range(TILES):
                        for kt in range(TILES):
                            ins = mm(o[:, m, t * P:(t + 1) * P], lhsT=v_tok[:, kt, hp * P:(hp + 1) * P],
                                     rhs=probT[:, 2 * (hp % 2) + m, t, kt, :], start=(kt == 0), stop=(kt == TILES - 1))
                end(ins, ("apv", hp))
                if hp < 2:
                    attention_scores(hp + 2)

            gate_next = [0]

            def fill(n=1):
                for _ in range(n):
                    i = gate_next[0]
                    if i < 12:
                        gate_next[0] += 1
                        o, w = begin_unit("gate", i)
                        for m in range(2):
                            for k in range(KT):
                                ins = mm(o[:, m, :], lhsT=w[:, k, m * P:(m + 1) * P], rhs=nT[:, k, :],
                                         start=(k == 0), stop=(k == KT - 1))
                        ins.then_inc(proj_full, 1)

            pe.wait_ge(sg["tilde_ok"], 1)
            for t in range(TILES):
                if t == 0:
                    for tt in range(TILES):
                        o = begin(("g", tt))
                        end(mm(o, lhsT=g_sig[:, tt * P:(tt + 1) * P], rhs=glora[:, :], start=True, stop=True), ("g", tt))
                for h in range(HEADS):
                    o = begin(("gram", t, h))
                    b0, cc = HD * (h % 2), h // 2
                    for i, src in enumerate((bb, kb)):
                        ins = mm(o[:, 256 * i:256 * i + 256].rearrange("p (a b) -> p a b", a=2),
                                 lhsT=src[b0:b0 + HD, cc, t * P:(t + 1) * P],
                                 rhs=ar[b0:b0 + HD, cc, :, t * P:(t + 1) * P], start=True, stop=True)
                    end(ins, ("gram", t, h))
                fill(1)
                for l in range(LEVELS):
                    for g in range(2):
                        o = begin(("A", t, l, g))
                        pe.wait_ge(sg["lm_ok"], 2 * (LEVELS * t + l) + g + 1)
                        if l == 1:
                            wait_read(pe, ("A", t, 0, g))
                            pe.wait_ge(sg["xt0"], 2 * t + g + 1)
                        if l > 1:
                            wait_read(pe, ("X", t, l - 1, g))
                        for i in range(4):
                            h = 4 * g + i
                            ins = mm(o[:, i * P:(i + 1) * P], lhsT=LmT[:, h, :],
                                     rhs=(X[:, h, :] if l else ident), start=True, stop=True)
                        end(ins, ("A", t, l, g))
                    if l < LEVELS - 1:
                        fill(1)
                    if l == 0:
                        continue
                    if l < LEVELS - 1:
                        for g in range(2):
                            o = begin(("X", t, l, g))
                            wait_read(pe, ("A", t, l, g))
                            if l > 1:
                                wait_read(pe, ("XT", t, l - 1, g))
                            for i in range(4):
                                h = 4 * g + i
                                ins = mm(o[:, i * P:(i + 1) * P], lhsT=XT[:, h, :], rhs=A1[:, h, :], start=True, stop=True)
                            end(ins, ("X", t, l, g))
                    for g in range(2):
                        o = begin(("XT", t, l, g))
                        wait_read(pe, ("A", t, l, g))
                        wait_read(pe, ("XT", t, l - 1, g)) if l > 1 else None
                        for i in range(4):
                            h = 4 * g + i
                            ins = mm(o[:, i * P:(i + 1) * P], lhsT=A1[:, h, :], rhs=XT[:, h, :], start=True, stop=True)
                        end(ins, ("XT", t, l, g))
                for g in range(2):
                    wait_read(pe, ("XT", t, LEVELS - 1, g))
                for n in (2 * t, 2 * t + 1):
                    e = n % 2
                    r0 = CHUNK * e
                    tc = slice(CHUNK * n, CHUNK * n + CHUNK)
                    tl = slice(r0, r0 + CHUNK)
                    o = begin(("rhs", n))
                    if n > 0:
                        wait_read(pe, ("S", n - 1))
                    for cc in range(CT):
                        cols = slice(cc * P, (cc + 1) * P)
                        if n > 0:
                            mm(o[tl, cols], lhsT=ar[:, cc, 0, tc], rhs=state[:, cc, :], start=True, stop=True,
                               skip_group_check=True)
                        for m in range(2):
                            h = 2 * cc + m
                            ins = mm(o[tl, h * HD:(h + 1) * HD], lhsT=gram[:, h, 2, tl], rhs=vtok[:, t, h * HD:(h + 1) * HD],
                                     start=(n == 0), stop=True, skip_group_check=True)
                    end(ins, ("rhs", n))
                    fill(1)
                    o = begin(("U", n))
                    wait_read(pe, ("rhs", n))
                    for h in range(HEADS):
                        ins = mm(o[tl, h * HD:(h + 1) * HD], lhsT=XT[:, h, tl], rhs=rhs_sb[:, h * HD:(h + 1) * HD],
                                 start=True, stop=True)
                    end(ins, ("U", n))
                    o = begin(("Y", n))
                    for cc in range(CT):
                        cols = slice(cc * P, (cc + 1) * P)
                        if n > 0:
                            mm(o[tl, cols], lhsT=ar[:, cc, 1, tc], rhs=state[:, cc, :], start=True, stop=True,
                               skip_group_check=True)
                        for m in range(2):
                            h = 2 * cc + m
                            hs = slice(h * HD, (h + 1) * HD)
                            mm(o[tl, hs], lhsT=gram[:, h, 3, tl], rhs=vtok[:, t, hs], start=(n == 0), stop=False,
                               skip_group_check=True)
                            if h == 0:
                                wait_read(pe, ("U", n))
                            ins = mm(o[tl, hs], lhsT=gram[:, h, 1, tl], rhs=U[:, hs], start=False, stop=True,
                                     skip_group_check=True)
                    end(ins, ("Y", n))
                    if n < NCHUNK - 1:
                        o = begin(("S", n))
                        for cc in range(CT):
                            cols = slice(cc * P, (cc + 1) * P)
                            mm(o[:, cols], lhsT=btok[tl, t, cols], rhs=U[tl, cols], start=True, stop=False)
                            ins = mm(o[:, cols], lhsT=ktok[tl, t, cols], rhs=vtok[tl, t, cols], start=False, stop=True)
                        end(ins, ("S", n))
                    fill(1)
                pe.wait_ge(sg["y_ready"], t + 1)
                transposes(("yt", t), [ytok[:, t, i * P:(i + 1) * P] for i in range(CT)])
            fill(12)
            wait_read(pe, ("yt", 1))
            wait_read(pe, ("yt", 0))
            wait_read(pe, ("apv", 3))
            ys = (y_att, y_rwkv, y_mem)
            for u in range(12):
                grp, br = u // 3, u % 3
                o, w = begin_unit("up", u, u // 2)
                for m in range(2):
                    for k in range(4):
                        ins = mm(o[:, m, :], lhsT=w[:, 4 * (u % 2) + k, m * P:(m + 1) * P], rhs=ys[br][:, k, :],
                                 start=(k == 0), stop=(k == 3))
                ins.then_inc(proj_full, 1)
            pe.wait_ge(sg["merged_ok"], 4)
            tokens("out", 4, merged)
            for t in range(TILES):
                pe.wait_ge(sg["xn_ok"], t + 1)
                for q in range(2):
                    transposes(("xn", t, q), [xn_tok[:, t, (4 * q + i) * P:(4 * q + i + 1) * P] for i in range(4)])
            for t in range(TILES):
                for q in range(2):
                    wait_read(pe, ("xn", t, q))
            for i in range(PEER_HEADS):
                o, w = begin_unit("peer_q", i)
                for m in range(2):
                    for k in range(KT):
                        ins = mm(o[:, m, :], lhsT=w[:, k, m * P:(m + 1) * P], rhs=xnT[:, k, :],
                                 start=(k == 0), stop=(k == KT - 1))
                ins.then_inc(proj_full, 1)
                if i > 0:
                    key_scores(pe, mm, begin, end, i - 1)
            key_scores(pe, mm, begin, end, PEER_HEADS - 1)
            for t in range(TILES):
                if t == 0:
                    wait_unit_read(pe, "peer_q", PEER_HEADS - 1)
                    wait_unit_read(pe, "peer_q", PEER_HEADS - 2)
                else:
                    pe.wait_ge(sg["o_sb_ok"], 2 * t)
                for d in range(2):
                    ins = mm(psum_proj[:, d, :], lhsT=ident, rhs=h_tok[:, t, 512 * d:512 * d + 512],
                             start=True, stop=True, skip_group_check=True)
                ins.then_inc(sg["h_done"], 1)
                with pe.Fori(0, PEER_HEADS // 2) as i:
                    for par in range(2):
                        for g in range(SLOTS // GROUP):
                            pe.wait_ge(sg["diag_ok"], i * 8 + (32 * t + 4 * par + g + 1))
                            for s in range(GROUP * g, GROUP * g + GROUP):
                                for d in range(2):
                                    ins = mm(psum_proj[:, d, :], lhsT=diag[:, s % (2 * GROUP), :],
                                             rhs=slot[s][:, D + 512 * d:D + 512 * d + 512],
                                             start=False, stop=True, skip_group_check=True)
                            ins.then_inc(sg["group_free"], 1)

        @block.scalar
        def _(act):
            st = Steps(act, act_step)
            A = nc.scalar.activation

            def norm_roots(base, s_in, need, done, scale, eps):
                act.wait_ge(s_in, need)
                A(sm(ROOT + base, 1), sm(SSQ + base, 1), ACT.Sqrt, scale=scale, bias=eps_col).then_inc(done, 1)

            act.wait_ge(sg["pads"], 1)
            for n in range(4):
                norm_roots(n, sg["ssq"], n + 1, sg["root"], 1.0 / D, EPS)
            act.wait_ge(sg["mix_pad"], 1)
            for i in range(7):
                wait_unit(act, "rwkv", i)
                unit_read(nc.scalar.copy(pT[:, 2 * i:2 * i + 2, 1:S + 1], halves(ubank("rwkv", i))), "rwkv", i)
            for i in range(2):
                wait_unit(act, "mem_k", i)
                nc.scalar.copy(kmT[:, 2 * i:2 * i + 2, :], halves(ubank("mem_k", i)))
                unit_read(A(mem_sq["mk"][:, 2 * i:2 * i + 2, :], halves(ubank("mem_k", i)), ACT.Square), "mem_k", i)
            act.wait_ge(sg["mixed_ok"], 7)
            st(A(w_tanh, mixed[0:64, 12, :], ACT.Tanh)).wait()
            A(g_sig, mixed[:, 13, :], ACT.Sigmoid).then_inc(sg["lora_in"], 1)
            for j, b, dst in (("wl", "w0", sgw), ("al", "a0", a_gate)):
                for i in range(2):
                    wait_job(act, (j, i))
                    for m in range(2):
                        ins = A(dst[:, 2 * i + m, :], bank((j, i))[:, m * S:(m + 1) * S], ACT.Sigmoid,
                                bias=v(b, 2 * i + m))
                    job_read(ins, (j, i))
            act.wait_ge(sg["kk_ok"], 1)
            A(knorm, kk, ACT.Square).then_inc(sg["kk2_ok"], 1)
            for i in range(2):
                wait_unit(act, "mem_v", i)
                unit_read(nc.scalar.copy(vm[:, :, 256 * i:256 * i + 256], halves(ubank("mem_v", i))), "mem_v", i)
            act.wait_ge(sg["lex_ok"], 1)
            st(A(p_inv, cum, ACT.Exp, scale=DECAY)).wait()
            st(A(cum, cum, ACT.Exp, scale=-DECAY))
            A(p_ex, p_ex, ACT.Exp, scale=-DECAY).then_inc(sg["decay_ok"], 1)
            wait_read(act, ("kn", 0))
            wait_read(act, ("kn", 1))
            A(knorm, knorm, ACT.Sqrt).then_inc(sg["kroot"], 1)
            for t in range(TILES):
                wait_job(act, ("vt", t))
                job_read(nc.scalar.copy(vtok[:, t, :], bank(("vt", t))), ("vt", t))
            for i in range(2):
                wait_unit(act, "mem_q", i)
                nc.scalar.copy(mqT[:, 2 * i:2 * i + 2, :], halves(ubank("mem_q", i)))
                unit_read(A(mem_sq["mq"][:, 2 * i:2 * i + 2, :], halves(ubank("mem_q", i)), ACT.Square), "mem_q", i)
            for x in ("mk", "mq"):
                for i in range(2):
                    wait_job(act, (x + "_ss", i))
                    job_read(A(mem_rn[x][:, 2 * i:2 * i + 2, :], halves(bank((x + "_ss", i))), ACT.Sqrt,
                               scale=1.0 / P, bias=eps_col), (x + "_ss", i))
            act.wait_ge(sg["trig_arg"], 2)
            A(trig[:, :, :], trig[:, :, :], ACT.Sin).then_inc(sg["trig_ok"], 1)
            wait_unit(act, "idx_q", 0)
            unit_read(nc.scalar.copy(iqT, halves(ubank("idx_q", 0))), "idx_q", 0)
            wait_unit(act, "idx_k", 0)
            st(nc.scalar.copy(ikT, ubank("idx_k", 0)[:, 0:S]))
            unit_read(nc.scalar.mul(sm(IW, 8), ubank("idx_k", 0)[:, S:S + 8], 1.0 / 16), "idx_k", 0)

            def raw_and_square(x, i):
                wait_unit(act, x, i)
                nc.scalar.copy(rope_raw[x][:, 2 * i:2 * i + 2, :], halves(ubank(x, i)))
                unit_read(A(rope_sq[x][:, 2 * i:2 * i + 2, :], halves(ubank(x, i)), ACT.Square), x, i)

            for i in range(2):
                raw_and_square("q", i)
            for j, dst in (("bt", btok), ("kt", ktok)):
                for t in range(TILES):
                    wait_job(act, (j, t))
                    job_read(nc.scalar.copy(dst[:, t, :], bank((j, t))), (j, t))
            for t in range(TILES):
                wait_job(act, ("bonus", t))
                job_read(nc.scalar.copy(sm(BON + 8 * t, 8), bank(("bonus", t))[:, 0:8]), ("bonus", t))
            for t in range(TILES):
                for hp in range(2):
                    wait_job(act, ("ms", t, hp))
                    act.wait_ge(sg["mmax"], 2 * t + hp + 1)
                    for m in range(2):
                        hh = 2 * hp + m
                        ins = A(mprob[:, t, hh, :], bank(("ms", t, hp))[:, m * S:(m + 1) * S], ACT.Exp,
                                scale=float(P) ** -0.5, bias=sm(NMX + 4 * t + hh), accum_out=sm(SU + 4 * t + hh))
                    job_read(ins, ("ms", t, hp))
            for i in range(2):
                raw_and_square("k", i)
            for t in range(TILES):
                for i in range(2):
                    wait_job(act, ("il", t, i))
                    if 2 * t + i > 0:
                        act.wait_ge(sg["relu_used"], 2 * t + i)
                    job_read(A(idx_relu, halves(bank(("il", t, i))), ACT.Relu), ("il", t, i))
            for i in range(2):
                wait_unit(act, "v", i)
                unit_read(nc.scalar.copy(v_tok[:, :, 256 * i:256 * i + 256], halves(ubank("v", i))), "v", i)
            for t in range(TILES):
                for hp in range(2):
                    wait_job(act, ("mpt", t, hp))
                    job_read(nc.scalar.copy(mprobT[:, t, 2 * hp:2 * hp + 2, :, :].rearrange("p a b c -> p (a b c)"),
                                            bank(("mpt", t, hp))), ("mpt", t, hp))
            for hp in range(2):
                wait_job(act, ("mpv", hp))
                job_read(nc.scalar.copy(y_mem[:, 2 * hp:2 * hp + 2, :], halves(bank(("mpv", hp)))), ("mpv", hp))
            for x in "qk":
                for i in range(2):
                    wait_job(act, (x + "_ss", i))
                    job_read(A(rope_rn[x][:, 2 * i:2 * i + 2, :], halves(bank((x + "_ss", i))), ACT.Sqrt,
                               scale=1.0 / HD, bias=eps_col), (x + "_ss", i))
            for hp in range(4):
                act.wait_ge(sg["amax"], hp + 1)
                for m in range(2):
                    for t in range(TILES):
                        ins = A(prob[:, 2 * (hp % 2) + t, m, :], prob[:, 2 * (hp % 2) + t, m, :], ACT.Exp,
                                bias=sm(NMX + 4 * (hp % 2) + 2 * t + m), accum_out=sm(SU + 4 * (hp % 2) + 2 * t + m))
                ins.then_inc(sg["aexp"], 1)

            gate_next = [0]

            def fill(n=1):
                for _ in range(n):
                    i = gate_next[0]
                    if i < 12:
                        gate_next[0] += 1
                        wait_unit(act, "gate", i)
                        for m in range(2):
                            ins = A(gates[:, 2 * i + m, :], ubank("gate", i)[:, m * S:(m + 1) * S], ACT.Sigmoid,
                                    bias=v("gate_bias", 2 * i + m))
                        unit_read(ins, "gate", i)

            act.wait_ge(sg["rope_ok"], 2)
            for t in range(TILES):
                if t == 0:
                    for tt in range(TILES):
                        wait_job(act, ("g", tt))
                        job_read(nc.scalar.copy(gtok[:, tt, :], bank(("g", tt))), ("g", tt))
                fill(1)
                for l in range(LEVELS):
                    for g in range(2):
                        if l > 0:
                            wait_job(act, ("A", t, l, g))
                            job_read(nc.scalar.copy(A1[:, 4 * g:4 * g + 4, :].rearrange("p a b -> p (a b)"),
                                                    bank(("A", t, l, g))), ("A", t, l, g))
                    if l < LEVELS - 1:
                        fill(1)
                for n in (2 * t, 2 * t + 1):
                    tl = slice(CHUNK * (n % 2), CHUNK * (n % 2) + CHUNK)
                    wait_job(act, ("rhs", n))
                    job_read(nc.scalar.copy(rhs_sb[tl, :], bank(("rhs", n))[tl, :]), ("rhs", n))
                    fill(1)
                    wait_job(act, ("U", n))
                    job_read(nc.scalar.copy(U[tl, :], bank(("U", n))[tl, :]), ("U", n))
                    wait_job(act, ("Y", n))
                    job_read(nc.scalar.copy(ytok[tl, t, :], bank(("Y", n))[tl, :]), ("Y", n))
                    fill(1)
                act.wait_ge(sg["gn_sq"], t + 1)
                A(sm(GN + 8, 8), sm(GN + 8, 8), ACT.Sqrt, scale=1.0 / HD, bias=gn_eps_col).then_inc(sg["gn_root"], 1)
                wait_job(act, ("yt", t))
                job_read(nc.scalar.copy(y_rwkv[:, :, t * P:(t + 1) * P],
                                        bank(("yt", t)).rearrange("p (a b) -> p a b", a=CT)), ("yt", t))
            fill(12)
            for t in range(TILES):
                act.wait_ge(sg["h_ssq"], t + 1)
                A(sm(HS + 2 + t), sm(HS + t), ACT.Sqrt, scale=1.0 / D, bias=eps_col).then_inc(sg["h_root"], 1)
            for t in range(TILES):
                for q in range(2):
                    wait_job(act, ("xn", t, q))
                    job_read(nc.scalar.copy(xnT[:, 4 * q:4 * q + 4, t * P:(t + 1) * P],
                                            bank(("xn", t, q)).rearrange("p (a b) -> p a b", a=4)), ("xn", t, q))
            sc4 = scores[:, 0:PEER_HEADS * TILES * 256].rearrange("p (t h k) -> p t h k", t=TILES, h=PEER_HEADS)
            for h in range(PEER_HEADS):
                wait_unit(act, "peer_q", h)
                if h >= 2:
                    wait_job(act, ("ps", h - 2))
                unit_read(nc.scalar.copy(qp[h % 2], halves(ubank("peer_q", h))), "peer_q", h)
                if h > 0:
                    wait_job(act, ("ps", h - 1))
                    job_read(nc.scalar.copy(sc4[:, :, h - 1, :], halves(bank(("ps", h - 1)))), ("ps", h - 1))
            h = PEER_HEADS - 1
            wait_job(act, ("ps", h))
            job_read(nc.scalar.copy(sc4[:, :, h, :], halves(bank(("ps", h)))), ("ps", h))
            last = JOB[("ps", h)]

            def stage_scores(n, par, need_used=None):
                if need_used is not None:
                    act.wait_ge(sg["stage_used"], need_used)
                nc.scalar.copy(stage[:, par].rearrange("p a b -> p (a b)"),
                               scores[:, bass.ds(n * 256, 256)] if not isinstance(n, int)
                               else scores[:, n * 256:(n + 1) * 256]).then_inc(sg["stage_ok"], 1)

            def soften(par, need):
                act.wait_ge(sg["gate_in"], need)
                A(gate_e[:, par, :], top[:, par, :], ACT.Exp, bias=gstat[:, par, 0:1],
                  accum_out=gstat[:, par, 1:2]).then_inc(sg["gsum"], 1)

            act.wait_ge(bank_free[last % BANKS], last // BANKS + 1)
            stage_scores(0, 0)
            stage_scores(1, 1)
            soften(0, 1)
            for t in range(TILES):
                with act.Fori(0, PEER_HEADS // 2) as i:
                    for par in range(2):
                        act.wait_ge(sg["stage_used"], i * 2 + (8 * t + par + 1))
                        stage_from = i * 512 + 256 * (8 * t + par + 2)
                        nc.scalar.copy(stage[:, par].rearrange("p a b -> p (a b)"),
                                       scores[:, bass.ds(stage_from, 256)]).then_inc(sg["stage_ok"], 1)
                        act.wait_ge(sg["gate_in"], i * 2 + (8 * t + par + 2))
                        A(gate_e[:, 1 - par, :], top[:, 1 - par, :], ACT.Exp, bias=gstat[:, 1 - par, 0:1],
                          accum_out=gstat[:, 1 - par, 1:2]).then_inc(sg["gsum"], 1)
                        for g in range(SLOTS // GROUP):
                            act.wait_ge(sg["dots"], i * 8 + (32 * t + 4 * par + g + 1))
                            A(act_h[:, par, GROUP * g:GROUP * g + GROUP], hid[:, par, GROUP * g:GROUP * g + GROUP],
                              ACT.Gelu).then_inc(sg["gelu_ok"], 1)
                act.wait_ge(sg["group_free"], 4 + 32 * (t + 1))
                if t > 0:
                    act.wait_ge(sg["stored"], 16 * t)
                for d in range(2):
                    nc.scalar.copy(o_sb[:, 512 * d:512 * d + 512], psum_proj[:, d, :]).then_inc(sg["o_sb_ok"], 1)

        @block.vector
        def _(dve):
            st = Steps(dve, dve_step)
            V = nc.vector
            dve.wait_ge(sg["pads"], 1)
            for n, (src, t) in enumerate([("x", 0), ("x", 1), ("mem", 0), ("mem", 1)]):
                if t == 0:
                    dve.wait_ge(tokens_in[src], 16)
                V.tensor_tensor_reduce(x_scaled[src][:, t, :], x_tok[src][:, t, :], x_tok[src][:, t, :], 1.0, 0.0, ALU.mult, ALU.add,
                                       sm(SSQ + n)).then_inc(sg["ssq"], 1)
                if n in (1, 3):
                    for k in (n - 1, n):
                        dve.wait_ge(sg["root"], k + 1)
                        st(V.reciprocal(sm(RSTD + k), sm(ROOT + k))).wait()
                        V.tensor_scalar(x_scaled[src][:, k % 2, :], x_tok[src][:, k % 2, :], sm(RSTD + k), None,
                                        ALU.mult).then_inc(sg["scaled"], 1)
                    if n == 1:
                        dve.wait_ge(params_in, 16 * 5)
                    dst, gain = (nT, "mix_gain") if src == "x" else (mT, "mem_gain")
                    for tt in range(TILES):
                        for q in range(2):
                            wait_job(dve, (src, tt, q))
                            job_read(V.tensor_tensor(
                                dst[:, 4 * q:4 * q + 4, tt * P:(tt + 1) * P],
                                bank((src, tt, q)).rearrange("p (a b) -> p a b", a=4),
                                v(gain, 4 * q, 4).unsqueeze(2).to_broadcast([P, 4, P]), ALU.mult), (src, tt, q))
            dve.wait_ge(sg["mix_pad"], 1)
            for i in range(7):
                wait_unit_read(dve, "rwkv", i)
                sl = slice(2 * i, 2 * i + 2)
                st(V.tensor_tensor(mixed[:, sl, :], pT[:, sl, 0:S], pT[:, sl, 1:S + 1], ALU.subtract)).wait()
                for m in range(2):
                    ins = V.scalar_tensor_tensor(mixed[:, 2 * i + m, :], mixed[:, 2 * i + m, :], v("mu", 2 * i + m),
                                                 pT[:, 2 * i + m, 1:S + 1], ALU.mult, ALU.add)
                ins.then_inc(sg["mixed_ok"], 1)
            dve.wait_ge(sg["mixed_ok"], 7)
            r_, k_ = mixed[:, 0:4, :], mixed[:, 4:8, :]
            for i in range(CT):
                V.tensor_scalar(kk[:, i, :], k_[:, i, :], v("k_k", i), None, ALU.mult)
            V.tensor_scalar(sm(OMKA, 4), v("k_a", 0, 4), -1.0, 1.0, ALU.mult, ALU.add).then_inc(sg["kk_ok"], 1)
            dve.wait_ge(sg["kk_ok"], 1)
            st(V.tensor_copy(trig[:, 0, :], pos_i[:, :])).wait()
            st(V.tensor_scalar(trig[:, 1, :], trig[:, 0, :], c("inv_freq"), None, ALU.mult)).wait()
            ang, turns, arg = trig[:, 1, :], work[:, 0, :], work[:, 1, :]
            MAGIC = 12582912.0
            C1, C2 = 6.28125, 0.0019340515136718750
            C3 = float(2 * np.pi - C1 - C2)
            for which, shift in ((0, 0.25), (1, 0.0)):
                st(V.tensor_scalar(turns, ang, float(1 / (2 * np.pi)), shift, ALU.mult, ALU.add)).wait()
                st(V.tensor_scalar(turns, turns, MAGIC, None, ALU.add)).wait()
                st(V.tensor_scalar(turns, turns, MAGIC, None, ALU.subtract)).wait()
                st(V.scalar_tensor_tensor(arg, turns, -C1, ang, ALU.mult, ALU.add)).wait()
                st(V.scalar_tensor_tensor(arg, turns, -C2, arg, ALU.mult, ALU.add)).wait()
                st(V.scalar_tensor_tensor(arg, turns, -C3, arg, ALU.mult, ALU.add)).wait()
                st(V.tensor_scalar(arg, arg, float(np.pi / 2) if which == 0 else 0.0, None, ALU.add)).wait()
                V.tensor_scalar(trig[:, which, :], arg, 3.1415925, -3.1415925, ALU.min, ALU.max).then_inc(
                    sg["trig_arg"], 1)
            wait_read(dve, ("wl", 0))
            wait_read(dve, ("wl", 1))
            for i in range(CT):
                st(V.tensor_tensor_scan(cum[:, i, :], reset, sgw[:, i, :], 0.0, ALU.mult, ALU.add))
            st.wait()
            V.tensor_tensor(p_ex, cum, sgw, ALU.subtract).then_inc(sg["lex_ok"], 1)
            for i in range(2):
                wait_job(dve, ("kn", i))
                job_read(V.tensor_scalar(knorm[:, 2 * i:2 * i + 2, :], halves(bank(("kn", i))), 1e-24, None, ALU.max),
                         ("kn", i))
            wait_read(dve, ("kn", 0))
            wait_read(dve, ("kn", 1))
            wait_read(dve, ("al", 0))
            wait_read(dve, ("al", 1))
            for i in range(CT):
                st(V.tensor_scalar(kmod[:, i, :], a_gate[:, i, :], v("k_a", i), sm(OMKA + i), ALU.mult, ALU.add))
            st.wait()
            st(V.tensor_tensor(kmod, kmod, k_, ALU.mult))
            dve.wait_ge(sg["kroot"], 1)
            st(V.reciprocal(knorm, knorm)).wait()
            st(V.tensor_tensor(kk, kk, knorm, ALU.mult)).wait()
            dve.wait_ge(sg["decay_ok"], 1)
            st(V.scalar_tensor_tensor(ar[:, :, 0, :], kk, -1.0, p_ex, ALU.mult, ALU.mult))
            st(V.tensor_tensor(ar[:, :, 1, :], r_, cum, ALU.mult))
            st(V.tensor_tensor(kk, kk, a_gate, ALU.mult)).wait()
            st(V.tensor_tensor(bb, kk, p_inv, ALU.mult))
            st(V.tensor_tensor(kb, kmod, p_inv, ALU.mult)).wait()
            p_end = cum.rearrange("p c (n k) -> p (c n) k", k=CHUNK)[:, :, CHUNK - 1:CHUNK]
            for dst, src in ((b_end, bb), (k_end, kb)):
                V.tensor_tensor(dst.rearrange("p c (n k) -> p (c n) k", k=CHUNK),
                                src.rearrange("p c (n k) -> p (c n) k", k=CHUNK),
                                p_end.to_broadcast([P, CT * NCHUNK, CHUNK]), ALU.mult).then_inc(sg["ends_ok"], 1)
            for i in range(CT):
                ins = V.scalar_tensor_tensor(rkk[:, i, :], r_[:, i, :], v("r_k", i), kmod[:, i, :], ALU.mult, ALU.mult)
                if i < CT - 1:
                    st(ins)
            ins.then_inc(sg["ends_ok"], 1)
            V.tensor_copy(pend, p_end.rearrange("p a b -> p (a b)")).then_inc(sg["tilde_ok"], 1)
            for x, dst in (("mk", kmT), ("mq", mqT)):
                wait_read(dve, (x + "_ss", 0))
                wait_read(dve, (x + "_ss", 1))
                st(V.reciprocal(mem_rn[x], mem_rn[x])).wait()
                V.scalar_tensor_tensor(dst, dst, v(x + "_gain"), mem_rn[x], ALU.mult, ALU.mult).then_inc(sg["mnorm_ok"], 1)

            def row_max(t, hp):
                wait_job(dve, ("ms", t, hp))
                st(V.tensor_reduce(sm(MX + 4 * t + 2 * hp, 2), halves(bank(("ms", t, hp))), AX, ALU.max)).wait()
                V.tensor_scalar(sm(NMX + 4 * t + 2 * hp, 2), sm(MX + 4 * t + 2 * hp, 2), -float(P) ** -0.5, None,
                                ALU.mult).then_inc(sg["mmax"], 1)

            for t in range(TILES):
                for hp in range(2):
                    row_max(t, hp)
            for t in range(TILES):
                wait_read(dve, ("ms", t, 0))
                wait_read(dve, ("ms", t, 1))
                st(V.reciprocal(sm(RS, 4), sm(SU + 4 * t, 4))).wait()
                ins = V.tensor_tensor(mprob[:, t], mprob[:, t], sm(RS, 4).unsqueeze(2).to_broadcast([P, 4, S]), ALU.mult)
                ins.then_inc(sg["mscaled"], 1)
                dve.wait_ge(sg["mscaled"], t + 1)
            dve.wait_ge(sg["trig_ok"], 1)
            wait_job(dve, ("iqrot", 0))
            cosb = trig[:, 0:1, :].to_broadcast([P, 2, S])
            sinb = trig[:, 1:2, :].to_broadcast([P, 2, S])
            st(V.tensor_tensor(iqT, iqT, cosb, ALU.mult))
            st(V.tensor_tensor(score, halves(bank(("iqrot", 0))), sinb, ALU.mult)).wait()
            job_read(V.tensor_tensor(iqT, iqT, score, ALU.add), ("iqrot", 0))
            wait_job(dve, ("ikrot", 0))
            st(V.tensor_tensor(ikT, ikT, trig[:, 0, :], ALU.mult))
            st(V.tensor_tensor(work[:, 0, :], bank(("ikrot", 0))[:, 0:S], trig[:, 1, :], ALU.mult)).wait()
            job_read(V.tensor_tensor(ikT, ikT, work[:, 0, :], ALU.add), ("ikrot", 0))
            wait_read(dve, ("ikrot", 0))
            wait_read(dve, ("iqrot", 0))
            for t in range(TILES):
                for i in range(2):
                    wait_read(dve, ("il", t, i))
                    for m in range(2):
                        hh = 2 * m + i
                        iw = sm(IW + 4 * t + hh)
                        if i == 0 and m == 0:
                            st(V.tensor_scalar(score[:, t, :], idx_relu[:, m, :], iw, None, ALU.mult)).wait()
                        else:
                            ins = V.scalar_tensor_tensor(score[:, t, :], idx_relu[:, m, :], iw, score[:, t, :],
                                                         ALU.mult, ALU.add)
                            if m == 0:
                                st(ins).wait()
                    ins.then_inc(sg["relu_used"], 1)
                    dve.wait_ge(sg["relu_used"], 2 * t + i + 1)
                near = slice(t * P, (t + 1) * P)
                st(V.tensor_tensor(score[:, t, near], score[:, t, near], c("causal"), ALU.add)).wait()
            for t in range(TILES):
                reach = slice(0, (t + 1) * P)
                for r in range(N_SEL // 8):
                    src = score[:, t, reach] if r == 0 else work[:, t, reach]
                    st(V.max(sm(MX, 8), src)).wait()
                    st(V.match_replace(work[:, t, reach], sm(MX, 8), src, TAKEN)).wait()
                st(V.tensor_scalar(work[:, t, reach], work[:, t, reach], TAKEN / 2, OFF, ALU.is_gt, ALU.mult))
                st(V.tensor_scalar(score[:, t, reach], score[:, t, reach], OFF / 2, OFF, ALU.is_lt, ALU.mult)).wait()
                st(V.tensor_tensor(bias[:, t, reach], work[:, t, reach], score[:, t, reach], ALU.add)).wait()
            st(V.memset(bias[:, 0, P:S], OFF)).wait()
            for n, (x, dst) in enumerate((("q", qT), ("k", kT))):
                wait_read(dve, (x + "_ss", 0))
                wait_read(dve, (x + "_ss", 1))
                st(V.reciprocal(rope_rn[x], rope_rn[x])).wait()
                V.scalar_tensor_tensor(rope_sq[x], rope_raw[x], v(x + "_gain"), rope_rn[x], ALU.mult,
                                       ALU.mult).then_inc(sg["rn_ok"], 1)
                dve.wait_ge(sg["rn_ok"], n + 1)
                st(V.tensor_tensor(dst, rope_sq[x], trig[:, 0:1, :].to_broadcast([P, CT, S]), ALU.mult))
                for i in range(2):
                    wait_job(dve, (x + "rot", i))
                    job_read(V.tensor_tensor(rope_raw[x][:, 2 * i:2 * i + 2, :], halves(bank((x + "rot", i))), sinb,
                                             ALU.mult), (x + "rot", i))
                wait_read(dve, (x + "rot", 0))
                wait_read(dve, (x + "rot", 1))
                st.wait()
                V.tensor_tensor(dst, dst, rope_raw[x], ALU.add).then_inc(sg["rope_ok"], 1)

            def attention_max(hp):
                for m in range(2):
                    wait_job(dve, ("as", hp, m))
                    for t in range(TILES):
                        p = prob[:, 2 * (hp % 2) + t, m, :]
                        ins = V.scalar_tensor_tensor(p, bank(("as", hp, m))[:, t * S:(t + 1) * S], HD ** -0.5,
                                                     bias[:, t, :], ALU.mult, ALU.add)
                    job_read(ins, ("as", hp, m))
                    wait_read(dve, ("as", hp, m))
                a = 4 * (hp % 2)
                st(V.tensor_reduce(sm(MX + a, 4), prob[:, 2 * (hp % 2):2 * (hp % 2) + 2, :, :].rearrange(
                    "p a b c -> p (a b) c"), AX, ALU.max)).wait()
                V.tensor_scalar(sm(NMX + a, 4), sm(MX + a, 4), -1.0, None, ALU.mult).then_inc(sg["amax"], 1)

            def attention_out(hp):
                for i in range(2):
                    wait_job(dve, ("apt", hp, i))
                    job_read(V.tensor_copy(probT[:, 2 * (hp % 2) + i].rearrange("p a b c -> p (a b c)"),
                                           bank(("apt", hp, i))), ("apt", hp, i))
                wait_job(dve, ("apv", hp))
                o = halves(bank(("apv", hp)))
                st(V.tensor_copy(y_att[0:64, hp, :], o[0:64, 0, :]))
                job_read(V.tensor_copy(y_att[64:128, hp, :], o[64:128, 1, :]), ("apv", hp))

            attention_max(0)
            for hp in range(4):
                a = 4 * (hp % 2)
                if hp < 3:
                    if hp > 0:
                        wait_job(dve, ("apt", hp - 1, 1))
                    attention_max(hp + 1)
                dve.wait_ge(sg["aexp"], hp + 1)
                st(V.reciprocal(sm(RS + a, 4), sm(SU + a, 4))).wait()
                pr = prob[:, 2 * (hp % 2):2 * (hp % 2) + 2, :, :].rearrange("p a b c -> p (a b) c")
                V.tensor_tensor(pr, pr, sm(RS + a, 4).unsqueeze(2).to_broadcast([P, 4, S]), ALU.mult
                                ).then_inc(sg["ascaled"], 1)
                attention_out(hp)

            for t in range(TILES):
                if t == 0:
                    st(V.memset(U, 0.0))
                    st(V.memset(rhs_sb, 0.0))
                    st(V.memset(state, 0.0)).wait()
                for h in range(HEADS):
                    wait_job(dve, ("gram", t, h))
                    if h == 0 and t == 0:
                        wait_read(dve, ("g", 1))
                    job_read(V.tensor_tensor(gram[:, h, :, :].rearrange("p a b -> p (a b)"), bank(("gram", t, h)),
                                             c("gram_mask"), ALU.mult), ("gram", t, h))
                for l in range(LEVELS):
                    for g in range(2):
                        gs = slice(4 * g, 4 * g + 4)
                        if l == 0:
                            wait_job(dve, ("A", t, 0, g))
                            job_read(V.tensor_tensor(X[:, gs, :], bank(("A", t, 0, g)).rearrange("p (a b) -> p a b", a=4),
                                                     ident.unsqueeze(1).to_broadcast([P, 4, P]), ALU.add), ("A", t, 0, g))
                            wait_read(dve, ("A", t, 0, g))
                    if 0 < l < LEVELS - 1:
                        for g in range(2):
                            gs = slice(4 * g, 4 * g + 4)
                            wait_job(dve, ("X", t, l, g))
                            job_read(V.tensor_tensor(X[:, gs, :].rearrange("p a b -> p (a b)"),
                                                     X[:, gs, :].rearrange("p a b -> p (a b)"), bank(("X", t, l, g)),
                                                     ALU.add), ("X", t, l, g))
                            wait_read(dve, ("X", t, l, g))
                    if l > 0:
                        for g in range(2):
                            gs = slice(4 * g, 4 * g + 4)
                            wait_job(dve, ("XT", t, l, g))
                            job_read(V.tensor_tensor(XT[:, gs, :].rearrange("p a b -> p (a b)"),
                                                     XT[:, gs, :].rearrange("p a b -> p (a b)"), bank(("XT", t, l, g)),
                                                     ALU.add), ("XT", t, l, g))
                            wait_read(dve, ("XT", t, l, g))
                for n in (2 * t, 2 * t + 1):
                    if n < NCHUNK - 1:
                        wait_job(dve, ("S", n))
                        pe_n = pend.rearrange("p (c n) -> p c n", n=NCHUNK)[:, :, n:n + 1]
                        for m in range(2):
                            r = slice(HD * m, HD * m + HD)
                            st(V.tensor_tensor(state[r, :, r], state[r, :, r], pe_n[r].to_broadcast([HD, CT, HD]),
                                               ALU.mult))
                        st.wait()
                        for m in range(2):
                            r = slice(HD * m, HD * m + HD)
                            ins = V.tensor_tensor(state[r, :, r], state[r, :, r],
                                                  bank(("S", n)).rearrange("p (a b) -> p a b", a=CT)[r, :, r], ALU.add)
                            if m == 0:
                                st(ins)
                        job_read(ins, ("S", n))
                        wait_read(dve, ("S", n))
                wait_read(dve, ("Y", 2 * t))
                wait_read(dve, ("Y", 2 * t + 1))
                y3 = ytok[:, t, :].rearrange("p (h i) -> p h i", h=HEADS)
                g3 = gn_tmp.rearrange("p (h i) -> p h i", h=HEADS)
                v3 = vtok[:, t, :].rearrange("p (h i) -> p h i", h=HEADS)
                st(V.tensor_reduce(sm(GN, 8), y3, AX, ALU.add)).wait()
                st(V.tensor_scalar(sm(GN, 8), sm(GN, 8), 1.0 / HD, None, ALU.mult)).wait()
                st(V.tensor_tensor(y3, y3, sm(GN, 8).unsqueeze(2).to_broadcast([P, 8, HD]), ALU.subtract)).wait()
                st(V.tensor_tensor(g3, y3, y3, ALU.mult)).wait()
                V.tensor_reduce(sm(GN + 8, 8), g3, AX, ALU.add).then_inc(sg["gn_sq"], 1)
                dve.wait_ge(sg["gn_root"], t + 1)
                st(V.tensor_tensor(g3, v3, sm(BON + 8 * t, 8).unsqueeze(2).to_broadcast([P, 8, HD]), ALU.mult))
                st(V.reciprocal(sm(GN + 16, 8), sm(GN + 8, 8))).wait()
                st(V.tensor_tensor(y3, y3, sm(GN + 16, 8).unsqueeze(2).to_broadcast([P, 8, HD]), ALU.mult)).wait()
                st(V.tensor_tensor(ytok[:, t, :], ytok[:, t, :], rows[:, 0:W], ALU.mult)).wait()
                st(V.tensor_tensor(ytok[:, t, :], ytok[:, t, :], rows[:, W:2 * W], ALU.add)).wait()
                st(V.tensor_tensor(ytok[:, t, :], ytok[:, t, :], gn_tmp, ALU.add)).wait()
                V.tensor_tensor(ytok[:, t, :], ytok[:, t, :], gtok[:, t, :], ALU.mult).then_inc(sg["y_ready"], 1)
                dve.wait_ge(sg["y_ready"], t + 1)
            wait_unit_read(dve, "gate", 11)
            wait_unit_read(dve, "gate", 10)
            for u in range(12):
                grp, br = u // 3, u % 3
                gt = gates[:, 8 * br + 2 * grp:8 * br + 2 * grp + 2, :]
                m2 = merged[:, 2 * grp:2 * grp + 2, :]
                wait_unit(dve, "up", u)
                if br == 0:
                    unit_read(V.tensor_tensor(m2, halves(ubank("up", u)), gt, ALU.mult), "up", u)
                    wait_unit_read(dve, "up", u)
                else:
                    unit_read(V.tensor_tensor(tmp_up, halves(ubank("up", u)), gt, ALU.mult), "up", u)
                    wait_unit_read(dve, "up", u)
                    ins = V.tensor_tensor(m2, m2, tmp_up, ALU.add)
                    if br == 2:
                        ins.then_inc(sg["merged_ok"], 1)
                        dve.wait_ge(sg["merged_ok"], grp + 1)
                    else:
                        st(ins).wait()
            dve.wait_ge(late_in, 48)
            for i in range(4):
                wait_unit(dve, "out", i)
                cols = slice(256 * i, 256 * i + 256)
                unit_read(V.tensor_tensor(h_tok[:, :, cols], halves(ubank("out", i)), x_again[:, :, cols], ALU.add), "out", i)
            wait_unit_read(dve, "out", 2)
            wait_unit_read(dve, "out", 3)
            for t in range(TILES):
                V.tensor_tensor_reduce(xn_tok[:, t, :], h_tok[:, t, :], h_tok[:, t, :], 1.0, 0.0, ALU.mult, ALU.add,
                                       sm(HS + t)).then_inc(sg["h_ssq"], 1)
            for t in range(TILES):
                dve.wait_ge(sg["h_root"], t + 1)
                st(V.reciprocal(sm(HS + 4 + t), sm(HS + 2 + t))).wait()
                V.scalar_tensor_tensor(xn_tok[:, t, :], h_tok[:, t, :], sm(HS + 4 + t), gain_row, ALU.mult,
                                       ALU.mult).then_inc(sg["xn_ok"], 1)

            def head(par, k):
                n = [0]

                def s(ins):
                    ins.then_inc(sg["choose"], 1)
                    n[0] += 1

                def w():
                    dve.wait_ge(sg["choose"], n[0])

                dve.sem_clear(sg["choose"])
                wait_alone(dve, sg["stage_ok"], k + 1)
                for half in range(2):
                    b8 = slice(8 * half, 8 * half + 8)
                    for side in range(2):
                        s(V.max(best[:, side, b8], stage[:, par, side, :]))
                    w()
                    for side in range(2):
                        s(V.max_index(best_i[:, side, b8], best[:, side, b8], stage[:, par, side, :]))
                    if half == 0:
                        w()
                        for side in range(2):
                            s(V.match_replace(stage[:, par, side, :], best[:, side, b8], stage[:, par, side, :], TAKEN))
                        w()
                w()
                V.tensor_copy(best_f[:, :, :], best_i[:, :, :]).then_inc(sg["stage_used"], 1)
                s(V.tensor_tensor(cand[:, :, :], best[:, 0, :].unsqueeze(2).to_broadcast([P, TOPK, TOPK]),
                                  best[:, 1, :].unsqueeze(1).to_broadcast([P, TOPK, TOPK]), ALU.add))
                w()
                dve.wait_ge(sg["stage_used"], k + 1)
                s(V.tensor_scalar(best_f[:, 0, :], best_f[:, 0, :], float(KEYS), None, ALU.mult))
                cf = cand[:, :, :].rearrange("p a b -> p (a b)")
                s(V.max(top[:, par, 0:8], cf)); w()
                s(V.max_index(top_i[:, 0:8], top[:, par, 0:8], cf))
                s(V.tensor_scalar(gstat[:, par, 0:1], top[:, par, 0:1], -1.0, None, ALU.mult)); w()
                s(V.match_replace(cf, top[:, par, 0:8], cf, TAKEN)); w()
                s(V.max(top[:, par, 8:16], cf)); w()
                V.max_index(top_i[:, 8:16], top[:, par, 8:16], cf).then_inc(sg["gate_in"], 1)
                dve.wait_ge(sg["gate_in"], k + 1)
                s(V.tensor_scalar(place_i[:, 0, :], top_i[:, :], 4, None, ALU.logical_shift_right))
                s(V.tensor_scalar(place_i[:, 1, :], top_i[:, :], 15, None, ALU.bitwise_and)); w()
                s(V.tensor_copy(place_f[:, :, :], place_i[:, :, :])); w()
                iota = c("iota").unsqueeze(1).to_broadcast([P, 2 * TOPK, TOPK])
                s(V.tensor_tensor(onehot[:, :, :], iota,
                                  place_f[:, :, :].rearrange("p a b -> p (a b)").unsqueeze(2).to_broadcast([P, 2 * TOPK, TOPK]),
                                  ALU.is_equal)); w()
                for side in range(2):
                    o = onehot[:, TOPK * side:TOPK * side + TOPK, :]
                    s(V.tensor_tensor(o, o, best_f[:, side:side + 1, :].to_broadcast([P, TOPK, TOPK]), ALU.mult))
                w()
                s(V.tensor_reduce(expert[:, :, :].rearrange("p a b -> p (a b)"), onehot[:, :, :], AX, ALU.add)); w()
                s(V.tensor_tensor(expert_f[:, :], expert[:, 0, :], expert[:, 1, :], ALU.add)); w()
                V.tensor_copy(expert_i[:, par, :], expert_f[:, :]).then_inc(sg["experts_ok"], 1)
                dve.wait_ge(sg["gsum"], k + 1)
                s(V.reciprocal(gstat[:, par, 2:3], gstat[:, par, 1:2])); w()
                V.tensor_scalar(gate_e[:, par, :], gate_e[:, par, :], gstat[:, par, 2:3], None, ALU.mult).then_inc(
                    sg["gate_ok"], 1)
            head(0, 0)
            for t in range(TILES):
                with dve.Fori(0, PEER_HEADS // 2) as i:
                    for par in range(2):
                        nh = i * 2 + (8 * t + par)
                        head(1 - par, nh + 1)
                        dve.wait_ge(sg["gate_ok"], nh + 1)
                        for g in range(SLOTS // GROUP):
                            for s_ in range(GROUP * g, GROUP * g + GROUP):
                                dve.wait_ge(slot_in[s_], nh * 16 + 16)
                                u = slot[s_][:, 0:D]
                                ins = V.tensor_tensor_reduce(u, u, xn_tok[:, t, :], 1.0, 0.0, ALU.mult, ALU.add,
                                                             hid[:, par, s_:s_ + 1])
                            ins.then_inc(sg["dots"], 1)
                            if g > 0:
                                diagonals(dve, V, nh * 4 + g, par, g - 1)
                        diagonals(dve, V, nh * 4 + 4, par, 3)

        @block.gpsimd
        def _(pool):
            st = Steps(pool, pool_step)
            G_ = nc.gpsimd
            G_.memset(eps_col, EPS)
            G_.memset(gn_eps_col, GN_EPS).then_inc(sg["pads"], 1)
            G_.memset(pT[:, :, 0:1], 0.0)
            st(G_.memset(reset, 1.0)).wait()
            G_.memset(reset.rearrange("p (n k) -> p n k", k=CHUNK)[:, :, 0:1], 0.0).then_inc(sg["mix_pad"], 1)
            for t in range(TILES):
                wait_read(pool, ("gram", t, HEADS - 1))
                if t > 0:
                    wait_job(pool, ("U", 2 * t - 1))
                for l in range(LEVELS):
                    level = const[:, CONST["level"][0] + l * P:CONST["level"][0] + (l + 1) * P]
                    for g in range(2):
                        gs = slice(4 * g, 4 * g + 4)
                        if l > 0:
                            wait_job(pool, ("A", t, l - 1, g))
                        if l == 1:
                            pool.wait_ge(sg["xt0"], 2 * t + g + 1)
                        G_.tensor_tensor(LmT[:, gs, :], gram[:, gs, 0, :], level.unsqueeze(1).to_broadcast([P, 4, P]),
                                         ALU.mult).then_inc(sg["lm_ok"], 1)
                    if l == 0:
                        for g in range(2):
                            gs = slice(4 * g, 4 * g + 4)
                            pool.wait_ge(sg["lm_ok"], 2 * LEVELS * t + g + 1)
                            G_.tensor_tensor(XT[:, gs, :], LmT[:, gs, :], ident.unsqueeze(1).to_broadcast([P, 4, P]),
                                             ALU.add).then_inc(sg["xt0"], 1)
            wait_job(pool, ("ps", PEER_HEADS - 1))
            pool.sem_inc(sg["group_free"], SLOTS // GROUP)
            with pool.Fori(0, PEER_HEADS * TILES // 2) as i:
                for par in range(2):
                    pool.wait_ge(sg["experts_ok"], i * 2 + (par + 1))
                    for s_ in range(SLOTS):
                        if s_ % GROUP == 0:
                            wait_alone(pool, sg["group_free"], i * 8 + (4 * par + s_ // GROUP + 1))
                        G_.indirect_dma_start(slot[s_], None, t_in["experts"],
                                              bass.IndirectOffsetOnAxis(ap=expert_i[:, par, s_:s_ + 1], axis=0)
                                              ).then_inc(slot_in[s_], 16)


def _cols(w, a, n):
    w = w[:, a:a + n]
    return w.reshape(w.shape[0] // P, P, n // 256, 256).transpose(2, 1, 0, 3)


def _vec(x):
    return np.asarray(x).reshape(-1, P).T


def kernel(**inputs):
    import concourse.bacc as bacc
    from concourse.bass_utils import run_bass_kernel_spmd

    a = {k: np.asarray(x) for k, x in inputs.items()}
    w_in = a["w_in"][0]
    pad = np.zeros((D, 124), np.float32)
    idx_k = np.concatenate([w_in[:, 1792:1856], w_in[:, 1792:1856], w_in[:, 1856:1860], pad], axis=1)
    w_up = a["w_up"][0].reshape(3, 4, P, 4, 256)
    up = w_up.transpose(3, 0, 2, 1, 4).reshape(6, 2, P, 4, 256).transpose(0, 2, 1, 3, 4).reshape(6, P, KT, 256)
    weights = np.concatenate([
        _cols(w_in, 1860, 1792), _cols(a["w_mem_kv"][0], 0, 512), _cols(a["w_mem_kv"][0], 512, 512),
        _cols(w_in, 3652, 512), _cols(w_in, 1536, 256), _cols(idx_k, 0, 256), _cols(w_in, 0, 512),
        _cols(w_in, 512, 512), _cols(w_in, 1024, 512), _cols(w_in, 4164, 3072), up,
        _cols(a["w_out"][0], 0, D), _cols(a["peer_w_q"][0], 0, 2048)]).reshape(BLOCKS, P, BLOCK)
    two = lambda x: np.concatenate([x, x])[:, None]
    vec = np.concatenate([
        _vec(a["mix_norm_gain"]), _vec(a["mem_norm_gain"]), _vec(a["gate_bias"]), _vec(a["rwkv_mu"]),
        _vec(a["rwkv_w0"]), _vec(a["rwkv_a0"]), _vec(a["rwkv_k_k"]), _vec(a["rwkv_k_a"]), _vec(a["rwkv_r_k"]),
        two(a["att_q_gain"][0]), two(a["att_k_gain"][0]), _vec(a["mem_q_gain"]), _vec(a["mem_k_gain"])], axis=1)
    arrays = {
        "x": a["x"][0], "mem": a["mem"][0], "positions": a["positions"].reshape(S), "const": constants(), "vec": vec,
        "lora": np.concatenate([a["rwkv_w2"][0], a["rwkv_a2"][0]]), "glora": a["rwkv_g2"][0],
        "rows": np.concatenate([a["rwkv_ln_w"][0], a["rwkv_ln_b"][0]]), "ffn_gain": a["ffn_norm_gain"][0],
        "keysT": np.stack([a["peer_key1"][0].T, a["peer_key2"][0].T], axis=1), "weights": weights,
        "experts": np.concatenate([a["peer_u"][0], a["peer_v"][0]], axis=1),
    }
    arrays = {"in_" + k: np.ascontiguousarray(x) for k, x in arrays.items()}
    nc = bacc.Bacc("TRN2", target_bir_lowering=False, num_devices=1)
    t_in = {k[3:]: nc.dram_tensor(k, x.shape, mybir.dt.from_np(x.dtype), kind="ExternalInput").ap()
            for k, x in arrays.items()}
    out = nc.dram_tensor("out", (S, D), F32, kind="ExternalOutput").ap()
    build(nc, t_in, out)
    r = run_bass_kernel_spmd(nc, [arrays], core_ids=[0])
    return r.results[0]["out"].reshape(1, S, D)
```

```python
from contextlib import ExitStack

import numpy as np
import concourse.bass as bass
from concourse import mybir

P = 128
D = 1024
S = 256
TILES = S // P
KT = D // P
W = 512
CT = W // P
HD = 64
HEADS = W // HD
CHUNK = 64
NCHUNK = S // CHUNK
MEM_HEADS = 4
N_SEL = 64
LEVELS = 6
PEER_HEADS = 8
TOPK = 16
KEYS = 128
EPS = 1e-6
GN_EPS = 64e-5
DECAY = float(np.exp(-0.5))
OFF = -1.0e30
TAKEN = -3.0e38
BLOCK = 2048
RING = 3
POOL_COLS = 187 * 256
SLOTS = 8
GROUP = 2
RING_GROUPS = SLOTS // GROUP
HEAD_GROUPS = TOPK // GROUP
QUERY_GROUPS = ((0, 0), (0, 0), (0, 0), (0, 0), (2, 2), (2, 2), (2, 2), (2, 2))

F32 = mybir.dt.float32
I32 = mybir.dt.int32
U32 = mybir.dt.uint32
ALU = mybir.AluOpType
ACT = mybir.ActivationFunctionType
AX = mybir.AxisListType.X

N_GATE0 = 2
N_GATE = 12 - N_GATE0
STREAM = [("rwkv", 7), ("mem_k", 2), ("mem_v", 2), ("mem_q", 2), ("idx_q", 1), ("idx_k", 1), ("v", 2),
          ("gate0", N_GATE0), ("q", 2), ("k", 2), ("gate", N_GATE), ("up", 6), ("out", 4), ("peer_q", 8)]
BLOCKS = sum(n for _, n in STREAM)
FIRST_BLOCK = {}
FIRST_UNIT = {}
_b = _u = 0
for _name, _n in STREAM:
    FIRST_BLOCK[_name], FIRST_UNIT[_name] = _b, _u
    _b += _n
    _u += _n * (2 if _name == "up" else 1)

CONST = {}
_c = 0
for _name, _n in [("ident", 128), ("headsel", 2), ("ones", 1), ("rot", 128), ("causal", 128),
                  ("gram_mask", 512), ("level", 128 * LEVELS), ("iota", 16), ("inv_freq", 1)]:
    CONST[_name] = (_c, _n)
    _c += _n
CONST_COLS = _c
FIRST_COLS = CONST["rot"][0]

VEC = {}
_c = 0
for _name, _n in [("mix_gain", 8), ("mem_gain", 8), ("gate_bias", 24), ("mu", 14), ("w0", 4), ("a0", 4),
                  ("k_k", 4), ("k_a", 4), ("r_k", 4), ("q_gain", 1), ("k_gain", 1), ("mq_gain", 1), ("mk_gain", 1), ("ffn_gain", 8)]:
    VEC[_name] = (_c, _n)
    _c += _n
VEC_COLS = _c


def constants():
    p = np.arange(P)
    out = {}
    out["ident"] = np.eye(P)
    out["ones"] = np.ones((P, 1))
    rot = np.zeros((P, P))
    for base in (0, HD):
        for i in range(8):
            rot[base + 8 + i, base + i] = -1.0
            rot[base + i, base + 8 + i] = 1.0
    out["rot"] = rot
    out["causal"] = np.where(p[None, :] <= p[:, None], 0.0, OFF)
    s, t = p[:, None], p[None, :]
    same = s // CHUNK == t // CHUNK
    strict, incl = same & (s < t), same & (s <= t)
    out["gram_mask"] = np.concatenate([strict, incl, strict, incl], axis=1)
    out["level"] = np.concatenate(
        [(s // (2 << l) == t // (2 << l)) & ((t >> l) % 2 == 1) & ((s >> l) % 2 == 0) for l in range(LEVELS)], axis=1)
    out["headsel"] = (p[:, None] // HD == np.arange(2)[None, :])
    out["iota"] = np.tile(np.arange(16), (P, 1))
    inv = (np.float32(1.0) / (np.float32(500000.0) ** (np.arange(0, 16, 2, dtype=np.float32) / np.float32(16))))
    col = np.zeros(P)
    for q in range(P):
        if q % HD < 16:
            col[q] = inv[(q % HD) % 8]
    out["inv_freq"] = col[:, None]
    return np.ascontiguousarray(np.concatenate([out[n] for n in CONST], axis=1).astype(np.float32))


SCHEDULE = [
    ("sumsq", "q"), ("gram", 0, 0), ("gate",), ("sumsq", "k"), ("gram", 0, 1), ("spread", "q"), ("spread", "k"),
    ("rope", "q"),
    ("inverse", 0, 0), ("rope", "k"), ("gate",), ("top", 0), ("inverse", 0, 1), ("gate",), ("top", 1),
    ("inverse", 0, 2), ("gate",), ("score", 0), ("inverse", 0, 3), ("exp", 0), ("score", 1), ("gate",), ("exp", 1),
    ("pair", 0), ("inverse", 0, 4), ("exp", 2), ("gate",), ("pair", 1), ("inverse", 0, 5), ("exp", 3), ("gate",),
    ("rhs", 0), ("pair", 2), ("u", 0), ("y", 0), ("gate",), ("rhs", 1), ("pair", 3), ("u", 1), ("y", 1), ("gram", 1, 0),
    ("gram", 1, 1), ("norm", 0), ("gate",), ("inverse", 1, 0), ("gate",), ("out", 0), ("inverse", 1, 1), ("inverse", 1, 2), ("inverse", 1, 3), ("up",), ("inverse", 1, 4), ("up",),
    ("inverse", 1, 5), ("up",), ("rhs", 2), ("up",), ("u", 2), ("y", 2), ("up",), ("rhs", 3), ("up",), ("u", 3), ("y", 3),
    ("norm", 1), ("up",), ("up",), ("out", 1),
]
assert SCHEDULE.count(("gate",)) == N_GATE and ("up",) not in SCHEDULE[:len(SCHEDULE) - SCHEDULE[::-1].index(("gate",))]
BRANCH_ORDER = (2, 0, 1)


SUMS = {"x": 1, "mem": 1, "kn": HEADS, "mk": MEM_HEADS, "mq": MEM_HEADS, "q": HEADS, "k": HEADS}


def spread_jobs(x):
    return [(x + "_rn", i) for i in range(1 if SUMS[x] == 1 else 2)]


def stage_jobs(stage):
    kind, a = stage[0], stage[1:]
    if kind == "sumsq":
        return [(a[0] + "_ss",)]
    if kind == "spread":
        return spread_jobs(a[0])
    if kind == "rope":
        return [(a[0] + "rot", i) for i in range(2)]
    if kind == "gram":
        return [("gram", a[0], h) for h in range(4 * a[1], 4 * a[1] + 4)]
    if kind == "inverse":
        t, l = a
        jobs = [("A", t, l, g) for g in range(2)]
        if 0 < l < LEVELS - 1:
            jobs += [("X", t, l, g) for g in range(2)]
        if l > 0:
            jobs += [("XT", t, l, g) for g in range(2)]
        return jobs
    if kind == "score":
        return [("as", a[0], m) for m in range(2)]
    if kind == "pair":
        return [("apt", a[0], i) for i in range(2)] + \
            ([("as", a[0] + 2, m) for m in range(2)] if a[0] < 2 else []) + [("apv", a[0])]
    if kind == "rhs":
        return [("rhs", a[0])]
    if kind == "u":
        return [("U", a[0])]
    if kind == "y":
        return [("Y", a[0])] + ([("S", a[0])] if a[0] < NCHUNK - 1 else [])
    if kind == "out":
        return [("yt", a[0])]
    return []


def job_plan():
    jobs = [("x_ss",)] + spread_jobs("x") + [("mem_ss",)] + spread_jobs("mem")
    jobs += [("mk_ss",)]
    jobs += [("wl", i) for i in range(2)] + [("al", i) for i in range(2)]
    jobs += [("vt", t) for t in range(TILES)]
    jobs += [("kn_ss",)]
    jobs += spread_jobs("kn") + [("mq_ss",)] + spread_jobs("mk") + spread_jobs("mq")
    jobs += [("iqrot", 0), ("ikrot", 0)]
    jobs += [("ms", t, hp) for t in range(TILES) for hp in range(2)]
    jobs += [("il", t, i) for t in range(TILES) for i in range(2)]
    jobs += [("bt", 0), ("bt", 1), ("kt", 0), ("kt", 1), ("bonus", 0), ("bonus", 1), ("g", 0), ("g", 1)]
    jobs += [("mpt", t, hp) for t in range(TILES) for hp in range(2)]
    jobs += [("mpv", hp) for hp in range(2)]
    for step in SCHEDULE:
        jobs += stage_jobs(step)
    jobs += [("ht", i) for i in range(4)]
    assert len(set(jobs)) == len(jobs)
    return {j: n for n, j in enumerate(jobs)}


JOB = job_plan()
BANKS = 6


def build(nc, t_in, out):
    ctx = ExitStack()
    with ctx:
        def sb(name, shape, dt=F32):
            return ctx.enter_context(nc.sbuf_tensor(name, shape, dt))

        def sem(name):
            return ctx.enter_context(nc.semaphore(name))

        const = sb("const", [P, CONST_COLS])
        vec = sb("vec", [P, VEC_COLS])
        trig = sb("trig", [P, 2, S])
        lora = sb("lora", [P, W])
        glora = sb("glora", [P, W])
        rows = sb("rows", [P, 2 * W])
        small = sb("small", [P, 160 + 16 * len(SUMS)])
        pos_i = sb("pos_i", [P, S], I32)
        pool_mem = sb("pool_mem", [P, POOL_COLS])

        def part(at, *shape):
            n = int(np.prod(shape))
            assert at + n <= POOL_COLS, (at, n)
            v = pool_mem[:, at:at + n]
            if len(shape) == 2:
                return v.rearrange("p (a b) -> p a b", a=shape[0])
            if len(shape) == 3:
                return v.rearrange("p (a b c) -> p a b c", a=shape[0], b=shape[1])
            if len(shape) == 4:
                return v.rearrange("p (a b c d) -> p a b c d", a=shape[0], b=shape[1], c=shape[2])
            return v

        K1 = 256
        G = 0
        gates = part(G, 24, S)
        h_tok = part(G, TILES, D)
        xn_tok = part(G + 8 * K1, TILES, D)
        N0 = G + 24 * K1
        nT = part(N0, KT, S)
        scores = part(G + 16 * K1, (PEER_HEADS * TILES + 2) * 256)
        E0 = N0 + 8 * K1
        iqT = part(E0, 2, S)
        ikT = part(E0 + 2 * K1, S)
        score = part(E0 + 3 * K1, TILES, S)
        work = part(E0 + 5 * K1, TILES, S)
        Y0 = E0 + 7 * K1
        y_att = part(Y0, CT, S)
        y_mem = part(Y0 + 4 * K1, CT, S)
        R0 = Y0 + 8 * K1
        wring = [part(R0 + BLOCK * i, KT, 256) for i in range(RING)]
        T0 = R0 + RING * BLOCK
        mT = part(T0, KT, S)
        kmT = part(T0 + 8 * K1, CT, S)
        vm = part(T0 + 12 * K1, TILES, W)
        mqT = part(T0 + 16 * K1, CT, S)
        mem_sq = {"mk": part(T0 + 20 * K1, CT, S), "mq": part(T0 + 28 * K1, CT, S)}
        mprob = part(T0 + 20 * K1, TILES, MEM_HEADS, S)
        mprobT = part(T0 + 28 * K1, TILES, MEM_HEADS, TILES, P)
        v_tok = part(T0, TILES, W)
        kT = part(T0 + 4 * K1, CT, S)
        qT = part(T0 + 8 * K1, CT, S)
        bias = part(T0 + 16 * K1, TILES, S)
        prob = part(T0 + 20 * K1, 4, 2, S)
        probT = part(T0 + 28 * K1, 4, 2, 2, P)
        merged = part(T0, KT, S)
        hT = part(T0 + 8 * K1, KT, S)
        tmp_up = part(T0 + 16 * K1, 2, S)
        Q0 = T0 + 36 * K1
        idx_relu = part(Q0 + 54 * K1, 2, S)
        in_sq = {"x": part(Q0, KT, S), "mem": part(Q0 + 8 * K1, KT, S)}
        ROPE0 = {"q": Q0 + 68 * K1, "k": T0 + 20 * K1}
        wide = {"kn": part(Q0 + 32 * K1, TILES, W), "q": part(ROPE0["q"] + 8 * K1, TILES, W),
                "k": part(ROPE0["k"] + 8 * K1, TILES, W)}
        x_rn = part(Q0 + 16 * K1, S)
        rope_raw = {x: part(a, CT, S) for x, a in ROPE0.items()}
        rope_sq = {x: part(a + 4 * K1, CT, S) for x, a in ROPE0.items()}
        ar = part(Q0, CT, 2, S)
        bb = part(Q0 + 8 * K1, CT, S)
        kb = part(Q0 + 12 * K1, CT, S)
        vtok = part(Q0 + 16 * K1, TILES, W)
        btok = part(Q0 + 20 * K1, TILES, W)
        ktok = part(Q0 + 24 * K1, TILES, W)
        kmod = part(Q0 + 28 * K1, CT, S)
        gtok = part(Q0 + 28 * K1, TILES, W)
        knorm = part(Q0 + 32 * K1, CT, S)
        ytok = part(Q0 + 32 * K1, TILES, W)
        mixed = part(Q0 + 36 * K1, 14, S)
        pT = part(Q0 + 50 * K1, 14, S + 1)
        sgw = part(Q0 + 50 * K1, CT, S)
        a_gate = part(Q0 + 54 * K1, CT, S)
        cum = part(Q0 + 58 * K1, CT, S)
        b_end = part(Q0 + 62 * K1, CT, S)
        k_end = part(Q0 + 50 * K1, CT, S)
        p_inv = part(Q0 + 68 * K1, CT, S)
        rkk = part(Q0 + 68 * K1, CT, S)
        p_ex = part(Q0 + 72 * K1, CT, S)
        kk = part(Q0 + 76 * K1, CT, S)
        gram = part(Q0 + 36 * K1, HEADS, 4, P)
        X = part(Q0 + 52 * K1, HEADS, P)
        XT = part(Q0 + 56 * K1, HEADS, P)
        A1 = part(Q0 + 60 * K1, HEADS, P)
        LmT = part(Q0 + 64 * K1, HEADS, P)
        y_rwkv = part(Q0 + 68 * K1, CT, S)
        state = part(Q0 + 72 * K1, CT, P)
        rhs_sb = part(Q0 + 74 * K1, W)
        U = part(Q0 + 76 * K1, W)
        gn_tmp = part(Q0 + 78 * K1, W)
        x_again = part(Q0, TILES, D)
        gain_row = part(Q0 + 8 * K1, D)
        qp = [part(Q0 + 12 * K1 + 512 * i, 2, S) for i in range(2)]
        keysT = part(T0 + 18 * K1, 2, KEYS)
        spare = [part(Y0, KT, 256), part(Q0, KT, 256), part(T0, KT, 256)]
        RING0 = Q0 + 16 * K1
        slot = [part(RING0 + BLOCK * i, BLOCK) for i in range(SLOTS)]
        o_sb = part(T0 + 20 * K1, D)

        at = [T0 + 24 * K1]

        def tail(dt, *shape):
            n = int(np.prod(shape))
            a = part(at[0], *shape) if dt == F32 else None
            if a is None:
                a = pool_mem[:, at[0]:at[0] + n].bitcast(dt)
                if len(shape) == 2:
                    a = a.rearrange("p (a b) -> p a b", a=shape[0])
            at[0] += n
            assert at[0] <= T0 + 36 * K1
            return a

        stage = tail(F32, 2, 2, KEYS)
        best = tail(F32, 2, TOPK)
        best_i = tail(U32, 2, TOPK)
        best_f = tail(F32, 2, TOPK)
        cand = tail(F32, TOPK, TOPK)
        top = tail(F32, 2, TOPK)
        top_i = tail(U32, TOPK)
        place_i = tail(U32, 2, TOPK)
        place_f = tail(F32, 2, TOPK)
        onehot = tail(F32, 2 * TOPK, TOPK)
        expert = tail(F32, 2, TOPK)
        expert_f = tail(F32, TOPK)
        expert_i = tail(U32, 2, TOPK)
        gate_e = tail(F32, 2, TOPK)
        gstat = tail(F32, 2, 4)
        hid = tail(F32, 2, TOPK)
        act_h = tail(F32, 2, TOPK)
        diag = tail(F32, 2 * GROUP, P)

        psum_proj = ctx.enter_context(nc.psum_tensor("psum_proj", [P, 2, 512], F32))
        psum_job = ctx.enter_context(nc.psum_tensor("psum_job", [P, BANKS, 512], F32))

        def c(name):
            a, n = CONST[name]
            return const[:, a:a + n]

        def v(name, i=0, n=1):
            a, _ = VEC[name]
            return vec[:, a + i:a + i + n]

        ident = c("ident")

        def sm(i, n=1):
            return small[:, i:i + n]
        OMKA = 12
        IW = 16
        BON = 24
        MX = 40
        SU = 56
        RS = 72
        GN = 88
        HS = 112
        NMX = 120
        EPSC = 118
        eps_col, gn_eps_col = sm(EPSC), sm(EPSC + 1)
        pend = sm(128, CT * NCHUNK)
        stat = {x: sm(160 + 16 * i, TILES * n) for i, (x, n) in enumerate(SUMS.items())}
        w_tanh = part(Q0 + 66 * K1, S)[0:64]
        g_sig = part(Q0 + 67 * K1, S)
        reset = part(E0 + 2 * K1, S)

        first_in, consts_in, vec_in, params_in = sem("first_in"), sem("consts_in"), sem("vec_in"), sem("params_in")
        tokens_in = {"x": sem("x_in"), "mem": sem("mem_in")}
        late_in = sem("late_in")
        weights_in = [sem(f"weights_in{i}") for i in range(RING)]
        proj_full = sem("proj_full")
        proj_free = [sem(f"proj_free{i}") for i in range(2)]
        bank_full = [sem(f"bank_full{i}") for i in range(BANKS)]
        bank_free = [sem(f"bank_free{i}") for i in range(BANKS)]
        dve_step, act_step, pool_step = sem("dve_step"), sem("act_step"), sem("pool_step")
        names = [
            "pads", "mix_pad", "ssq", "x_gained", "n_ok", "mixed_ok",
            "lora_in", "kk_ok", "kk2_ok", "kroot", "lex_ok", "decay_ok", "ends_ok", "tilde_ok",
            "trig_arg", "trig_ok", "mmax", "mscaled", "relu_used",
            "rope_ok", "amax", "aexp", "ascaled",
            "lm_ok", "xt0", "cleared", "gn_sq", "gn_root", "y_ready",
            "merged_ok", "h_ssq", "h_root", "h_rstd", "xn_ok",
            "ps_full", "ps_free", "stage_ok", "stage_used", "choose", "experts_ok", "gate_in", "gsum", "gate_ok",
            "dots", "gelu_ok", "diag_ok", "group_free", "o_sb_ok", "stored"]
        sg = {n: sem("s_" + n) for n in names}
        rms_ok = {x: sem("rms_ok_" + x) for x in SUMS}
        carried = {nc.vector.engine: sem("carried_dve"), nc.gpsimd.engine: sem("carried_pool")}
        spare_in = [sem(f"spare_in{i}") for i in range(3)]
        slot_in = [sem(f"slot_in{i}") for i in range(SLOTS)]

        def query_weights(i):
            if 3 <= i < 6:
                return spare[i - 3], spare_in[i - 3], 16
            b = FIRST_BLOCK["peer_q"] + i % 3
            return wring[b % RING], weights_in[b % RING], 16 * (b // RING + 1 + i // 6)

        class Steps:
            def __init__(self, eng, s):
                self.eng, self.s, self.n = eng, s, 0

            def __call__(self, ins):
                ins.then_inc(self.s, 1)
                self.n += 1
                return self

            def wait(self):
                self.eng.wait_ge(self.s, self.n)

        def bank(job):
            return psum_job[:, JOB[job] % BANKS, :]

        def wait_job(eng, job):
            eng.wait_ge(bank_full[JOB[job] % BANKS], JOB[job] // BANKS + 1)

        def job_read(ins, job):
            return ins.then_inc(bank_free[JOB[job] % BANKS], 1)

        def wait_read(eng, job):
            eng.wait_ge(bank_free[JOB[job] % BANKS], JOB[job] // BANKS + 1)

        def unit(name, i):
            return FIRST_UNIT[name] + i

        def ubank(name, i):
            return psum_proj[:, unit(name, i) % 2, :]

        def wait_unit(eng, name, i):
            eng.wait_ge(proj_full, unit(name, i) + 1)

        def unit_read(ins, name, i):
            return ins.then_inc(proj_free[unit(name, i) % 2], 1)

        def wait_unit_read(eng, name, i):
            eng.wait_ge(proj_free[unit(name, i) % 2], unit(name, i) // 2 + 1)

        def wait_alone(eng, s, value):
            eng.wait_ge(s, value)
            eng.sem_inc(carried[eng.engine], 1)

        def halves(ap):
            return ap.rearrange("p (a b) -> p a b", a=2)

        def score_bank(h):
            return psum_job[:, h % 2, :]

        def sum_bank(t, d):
            return psum_job[:, 2 + 2 * t + d, :]

        def key_scores(pe, mm, h):
            wait_unit_read(pe, "peer_q", h)
            if h == 0:
                pe.wait_ge(late_in, 48)
            if h >= 2:
                pe.wait_ge(sg["ps_free"], h - 1)
            o = score_bank(h)
            for t in range(TILES):
                for m in range(2):
                    ins = mm(o[:, (2 * t + m) * KEYS:(2 * t + m + 1) * KEYS], lhsT=qp[h % 2][:, m, t * P:(t + 1) * P],
                             rhs=keysT[:, m, :], start=True, stop=True)
            ins.then_inc(sg["ps_full"], 1)

        def diagonals(dve, V, done, par, g):
            dve.wait_ge(sg["gelu_ok"], done)
            dve.wait_ge(sg["group_free"], done + RING_GROUPS - 2)
            for s_ in range(GROUP * g, GROUP * g + GROUP):
                ins = V.tensor_scalar(diag[:, s_ % (2 * GROUP), :], ident, act_h[:, par, s_:s_ + 1],
                                      gate_e[:, par, s_:s_ + 1], ALU.mult, ALU.mult)
            ins.then_inc(sg["diag_ok"], 1)

        block = ctx.enter_context(nc.Block())

        @block.sync
        def _(sp):
            sp.dma_start(nT.rearrange("p a b -> p (a b)"), t_in["xT"]).then_inc(tokens_in["x"], 16)
            sp.dma_start(const[:, 0:FIRST_COLS], t_in["const"][:, 0:FIRST_COLS]).then_inc(first_in, 16)
            sp.dma_start(vec[:, :], t_in["vec"]).then_inc(vec_in, 16)
            for b in range(RING):
                sp.dma_start(wring[b].rearrange("p a b -> p (a b)"), t_in["weights"][b]).then_inc(weights_in[b], 16)
                if b == 1:
                    sp.dma_start(mT.rearrange("p a b -> p (a b)"), t_in["memT"]).then_inc(tokens_in["mem"], 16)
            sp.dma_start(const[:, FIRST_COLS:], t_in["const"][:, FIRST_COLS:]).then_inc(consts_in, 16)
            sp.dma_start(pos_i[:, :], t_in["positions"].partition_broadcast(P)).then_inc(params_in, 16)
            sp.dma_start(lora[:, :], t_in["lora"]).then_inc(params_in, 16)
            sp.dma_start(glora[:, :], t_in["glora"]).then_inc(params_in, 16)
            sp.dma_start(rows[:, :], t_in["rows"].partition_broadcast(P)).then_inc(params_in, 16)

            def load_query(i, s, value):
                w, arrived, _ = query_weights(i)
                sp.wait_ge(s, value)
                sp.dma_start(w.rearrange("p a b -> p (a b)"), t_in["weights"][FIRST_BLOCK["peer_q"] + i]).then_inc(
                    arrived, 16)

            steady = FIRST_BLOCK["up"] // RING
            with sp.Fori(1, steady) as i:
                for b in range(RING):
                    sp.wait_ge(proj_full, i * RING + (b - RING + 1))
                    sp.dma_start(wring[b].rearrange("p a b -> p (a b)"),
                                 t_in["weights"][bass.ds(i * RING + b, 1)].rearrange("o p n -> (o p) n")
                                 ).then_inc(weights_in[b], 16)
            for b in range(steady * RING, FIRST_BLOCK["peer_q"] + 3):
                old = b - RING
                last = old + 1
                if old >= FIRST_BLOCK["up"]:
                    last = FIRST_UNIT["up"] + 2 * min(old - FIRST_BLOCK["up"] + 1, 6) \
                        + max(old - FIRST_BLOCK["out"] + 1, 0)
                sp.wait_ge(proj_full, last)
                sp.dma_start(wring[b % RING].rearrange("p a b -> p (a b)"),
                             t_in["weights"][b]).then_inc(weights_in[b % RING], 16)
                if b == FIRST_BLOCK["out"]:
                    load_query(3, proj_full, FIRST_UNIT["up"] + 8)
            load_query(5, proj_full, FIRST_UNIT["out"] + 4)
            for i in (2, 3):
                wait_unit_read(sp, "out", i)
            load_query(4, proj_full, FIRST_UNIT["out"] + 4)
            for i in (6, 7):
                load_query(i, proj_full, FIRST_UNIT["peer_q"] + i - 5)
            for t in range(TILES):
                sp.wait_ge(sg["o_sb_ok"], 2 * t + 2)
                sp.dma_start(out[t * P:(t + 1) * P, :], o_sb).then_inc(sg["stored"], 16)
            sp.wait_ge(sg["stored"], 16 * TILES)

        @block.tensor
        def _(pe):
            mm, tr = nc.tensor.matmul, nc.tensor.transpose

            def begin(job):
                n = JOB[job]
                if n >= BANKS:
                    pe.wait_ge(bank_free[n % BANKS], n // BANKS)
                return psum_job[:, n % BANKS, :]

            def end(ins, job):
                ins.then_inc(bank_full[JOB[job] % BANKS], 1)

            def begin_unit(name, i, b=None):
                u = unit(name, i)
                blk = FIRST_BLOCK[name] + (i if b is None else b)
                w, arrived, count = wring[blk % RING], weights_in[blk % RING], 16 * (blk // RING + 1)
                if name == "peer_q":
                    w, arrived, count = query_weights(i)
                pe.wait_ge(arrived, count)
                if u >= 2:
                    pe.wait_ge(proj_free[u % 2], u // 2)
                return halves(psum_proj[:, u % 2, :]), w

            def channels(name, n, src, first=0, between=None):
                for i in range(first, n):
                    o, w = begin_unit(name, i)
                    for m in range(2):
                        for k in range(KT):
                            ins = mm(o[:, m, :], lhsT=w[:, k, m * P:(m + 1) * P], rhs=src[:, k, :],
                                     start=(k == 0), stop=(k == KT - 1))
                        if m == 1:
                            ins.then_inc(proj_full, 1)
                        elif between is not None:
                            between()

            def tokens(name, n, src, first=0):
                for i in range(first, n):
                    o, w = begin_unit(name, i)
                    for t in range(TILES):
                        for k in range(KT):
                            ins = mm(o[:, t, :], lhsT=src[:, k, t * P:(t + 1) * P], rhs=w[:, k, :],
                                     start=(k == 0), stop=(k == KT - 1))
                    ins.then_inc(proj_full, 1)

            def transposes(job, srcs):
                o = begin(job)
                for i, s in enumerate(srcs):
                    ins = tr(o[:, i * P:(i + 1) * P], s, ident)
                end(ins, job)

            def square_sums(x, sq, tiles=range(TILES)):
                n = SUMS[x]
                w = n // CT
                o = begin((x + "_ss",)) if tiles[0] == 0 else bank((x + "_ss",))
                for t in tiles:
                    if n == 1:
                        for k in range(KT):
                            ins = mm(o[:, t:t + 1], lhsT=sq[:, k, t * P:(t + 1) * P], rhs=c("ones"),
                                     start=(k == 0), stop=(k == KT - 1))
                    else:
                        for k in range(CT):
                            ins = mm(o[:, n * t + w * k:n * t + w * k + w], lhsT=sq[:, k, t * P:(t + 1) * P],
                                     rhs=c("ones") if w == 1 else c("headsel"), start=True, stop=True)
                if tiles[-1] == TILES - 1:
                    end(ins, (x + "_ss",))

            def spread(x):
                n = SUMS[x]
                w = max(n // CT, 1)
                pe.wait_ge(rms_ok[x], 1)
                for i, job in enumerate(spread_jobs(x)):
                    o = begin(job)
                    for m in range(1 if n == 1 else 2):
                        for t in range(TILES):
                            k = 2 * i + m
                            src = wide[x][:, t, k * P:(k + 1) * P] if w > 1 else \
                                stat[x][:, n * t + k:n * t + k + 1].to_broadcast([P, P])
                            ins = tr(o[:, m * S + t * P:m * S + t * P + P], src, ident)
                    end(ins, job)

            pe.wait_ge(sg["x_gained"], 2)
            channels("rwkv", 1, nT)
            pe.wait_ge(first_in, 16)
            square_sums("x", in_sq["x"])
            channels("rwkv", 2, nT, 1)
            spread("x")
            channels("rwkv", 3, nT, 2)
            pe.wait_ge(sg["ssq"], 4)
            square_sums("mem", in_sq["mem"], (0,))
            channels("rwkv", 4, nT, 3)
            square_sums("mem", in_sq["mem"], (1,))
            channels("rwkv", 5, nT, 4)
            spread("mem")
            channels("rwkv", 7, nT, 5)
            wait_read(pe, ("mem_rn", 0))
            channels("mem_k", 2, mT)
            tokens("mem_v", 2, mT)
            for i in range(2):
                wait_unit_read(pe, "mem_k", i)
            square_sums("mk", mem_sq["mk"])
            pe.wait_ge(consts_in, 16)
            pe.wait_ge(params_in, 16 * 4)
            pe.wait_ge(sg["lora_in"], 1)
            for j, r0, src in (("wl", 0, w_tanh), ("al", 64, mixed[64:128, 12, :])):
                for i in range(2):
                    o = halves(begin((j, i)))
                    for m in range(2):
                        cc = 2 * i + m
                        ins = mm(o[:, m, :], lhsT=lora[r0:r0 + 64, cc * P:(cc + 1) * P], rhs=src, start=True, stop=True)
                    end(ins, (j, i))
            pe.wait_ge(sg["mixed_ok"], 7)
            for t in range(TILES):
                transposes(("vt", t), [mixed[:, 8 + i, t * P:(t + 1) * P] for i in range(CT)])
            pe.wait_ge(sg["kk2_ok"], 1)
            square_sums("kn", knorm)
            pe.wait_ge(sg["n_ok"], 1)
            channels("mem_q", 2, nT)
            spread("kn")
            for i in range(2):
                wait_unit_read(pe, "mem_q", i)
            square_sums("mq", mem_sq["mq"])
            channels("idx_q", 1, nT)
            o, w = begin_unit("idx_k", 0)
            for t in range(TILES):
                for k in range(KT):
                    ins = mm(o[:, 1, 4 * t:4 * t + 4], lhsT=nT[:, k, t * P:(t + 1) * P], rhs=w[:, k, P:P + 4],
                             start=(k == 0), stop=(k == KT - 1))
                if t == 0:
                    for k in range(KT):
                        mm(o[:, 0, :], lhsT=w[:, k, 0:P], rhs=nT[:, k, :], start=(k == 0), stop=(k == KT - 1))
            ins.then_inc(proj_full, 1)
            tokens("v", 2, nT)
            spread("mk")
            spread("mq")
            wait_unit_read(pe, "idx_q", 0)
            o = begin(("iqrot", 0))
            end(mm(o, lhsT=c("rot"), rhs=iqT.rearrange("p a b -> p (a b)"), start=True, stop=True), ("iqrot", 0))
            wait_unit_read(pe, "idx_k", 0)
            o = begin(("ikrot", 0))
            end(mm(o[:, 0:S], lhsT=c("rot"), rhs=ikT, start=True, stop=True), ("ikrot", 0))
            channels("gate0", 1, nT)
            for job in spread_jobs("mk") + spread_jobs("mq"):
                wait_read(pe, job)
            for t in range(TILES):
                for hp in range(2):
                    o = halves(begin(("ms", t, hp)))
                    for m in range(2):
                        hh = 2 * hp + m
                        ins = mm(o[:, m, :], lhsT=mqT[:, hh, t * P:(t + 1) * P], rhs=kmT[:, hh, :], start=True, stop=True)
                    end(ins, ("ms", t, hp))
            wait_read(pe, ("iqrot", 0))
            wait_read(pe, ("ikrot", 0))
            for t in range(TILES):
                for i in range(2):
                    o = halves(begin(("il", t, i)))
                    for m in range(2):
                        ins = mm(o[:, m, :], lhsT=iqT[64 * i:64 * i + 64, m, t * P:(t + 1) * P],
                                 rhs=ikT[64 * i:64 * i + 64, :], start=True, stop=True)
                    end(ins, ("il", t, i))
            pe.wait_ge(sg["ends_ok"], 3)
            for j, src in (("bt", b_end), ("kt", k_end)):
                for t in range(TILES):
                    transposes((j, t), [src[:, i, t * P:(t + 1) * P] for i in range(CT)])
                if j == "bt":
                    channels("gate0", N_GATE0, nT, 1)
            for t in range(TILES):
                o = begin(("bonus", t))
                for i in range(CT):
                    ins = mm(o[:, 2 * i:2 * i + 2], lhsT=rkk[:, i, t * P:(t + 1) * P], rhs=c("headsel"),
                             start=True, stop=True)
                end(ins, ("bonus", t))
            pe.wait_ge(sg["tilde_ok"], 1)
            for t in range(TILES):
                o = begin(("g", t))
                end(mm(o, lhsT=g_sig[:, t * P:(t + 1) * P], rhs=glora[:, :], start=True, stop=True), ("g", t))
            channels("q", 2, nT)
            for t in range(TILES):
                pe.wait_ge(sg["mscaled"], t + 1)
                for hp in range(2):
                    transposes(("mpt", t, hp), [mprob[:, t, 2 * hp + i // 2, (i % 2) * P:(i % 2 + 1) * P] for i in range(4)])
            for hp in range(2):
                o = halves(begin(("mpv", hp)))
                for t in range(TILES):
                    wait_read(pe, ("mpt", t, hp))
                for m in range(2):
                    hh = 2 * hp + m
                    for t in range(TILES):
                        for mt in range(TILES):
                            ins = mm(o[:, m, t * P:(t + 1) * P], lhsT=vm[:, mt, hh * P:(hh + 1) * P],
                                     rhs=mprobT[:, t, hh, mt, :], start=(mt == 0), stop=(mt == TILES - 1))
                end(ins, ("mpv", hp))
            channels("k", 2, nT)

            def sumsq(x):
                wait_unit_read(pe, x, 0)
                wait_unit_read(pe, x, 1)
                square_sums(x, rope_sq[x])

            def rope(x):
                for job in spread_jobs(x):
                    wait_read(pe, job)
                for i in range(2):
                    o = begin((x + "rot", i))
                    end(mm(o, lhsT=c("rot"), rhs=rope_sq[x][:, 2 * i:2 * i + 2, :].rearrange("p a b -> p (a b)"),
                           start=True, stop=True), (x + "rot", i))

            def attention_scores(hp):
                if hp == 0:
                    pe.wait_ge(sg["rope_ok"], 2)
                for m in range(2):
                    o = halves(begin(("as", hp, m)))
                    for t in range(TILES):
                        ins = mm(o[:, t, :], lhsT=qT[64 * m:64 * m + 64, hp, t * P:(t + 1) * P],
                                 rhs=kT[64 * m:64 * m + 64, hp, :], start=True, stop=True)
                    end(ins, ("as", hp, m))

            def attention_pair(hp):
                pe.wait_ge(sg["ascaled"], hp + 1)
                for i in range(2):
                    transposes(("apt", hp, i), [prob[:, 2 * (hp % 2) + t, i, kt * P:(kt + 1) * P]
                                                for t in range(TILES) for kt in range(TILES)])
                if hp < 2:
                    attention_scores(hp + 2)
                o = halves(begin(("apv", hp)))
                wait_read(pe, ("apt", hp, 0))
                wait_read(pe, ("apt", hp, 1))
                if hp == 0:
                    wait_unit_read(pe, "v", 0)
                    wait_unit_read(pe, "v", 1)
                for m in range(2):
                    for t in range(TILES):
                        for kt in range(TILES):
                            ins = mm(o[:, m, t * P:(t + 1) * P], lhsT=v_tok[:, kt, hp * P:(hp + 1) * P],
                                     rhs=probT[:, 2 * (hp % 2) + m, t, kt, :], start=(kt == 0), stop=(kt == TILES - 1))
                end(ins, ("apv", hp))

            def gram_matrices(t, g):
                for h in range(4 * g, 4 * g + 4):
                    o = begin(("gram", t, h))
                    b0, cc = HD * (h % 2), h // 2
                    for i, src in enumerate((bb, kb)):
                        ins = mm(o[:, 256 * i:256 * i + 256].rearrange("p (a b) -> p a b", a=2),
                                 lhsT=src[b0:b0 + HD, cc, t * P:(t + 1) * P],
                                 rhs=ar[b0:b0 + HD, cc, :, t * P:(t + 1) * P], start=True, stop=True)
                    end(ins, ("gram", t, h))

            def inverse(t, l):
                for g in range(2):
                    o = begin(("A", t, l, g))
                    pe.wait_ge(sg["lm_ok"], 2 * (LEVELS * t + l) + g + 1)
                    if l == 1:
                        wait_read(pe, ("A", t, 0, g))
                        pe.wait_ge(sg["xt0"], 2 * t + g + 1)
                    if l > 1:
                        wait_read(pe, ("X", t, l - 1, g))
                    for i in range(4):
                        h = 4 * g + i
                        if l == 0:
                            ins = tr(o[:, i * P:(i + 1) * P], LmT[:, h, :], ident)
                        else:
                            ins = mm(o[:, i * P:(i + 1) * P], lhsT=LmT[:, h, :], rhs=X[:, h, :], start=True, stop=True)
                    end(ins, ("A", t, l, g))
                if 0 < l < LEVELS - 1:
                    for g in range(2):
                        o = begin(("X", t, l, g))
                        wait_read(pe, ("A", t, l, g))
                        if l > 1:
                            wait_read(pe, ("XT", t, l - 1, g))
                        for i in range(4):
                            h = 4 * g + i
                            ins = mm(o[:, i * P:(i + 1) * P], lhsT=XT[:, h, :], rhs=A1[:, h, :], start=True, stop=True)
                        end(ins, ("X", t, l, g))
                if l > 0:
                    for g in range(2):
                        o = begin(("XT", t, l, g))
                        wait_read(pe, ("A", t, l, g))
                        if l > 1:
                            wait_read(pe, ("XT", t, l - 1, g))
                        for i in range(4):
                            h = 4 * g + i
                            ins = mm(o[:, i * P:(i + 1) * P], lhsT=A1[:, h, :], rhs=XT[:, h, :], start=True, stop=True)
                        end(ins, ("XT", t, l, g))

            def chunk_cols(n):
                r0 = CHUNK * (n % 2)
                return n // 2, slice(CHUNK * n, CHUNK * n + CHUNK), slice(r0, r0 + CHUNK)

            def chunk_rhs(n):
                t, tc, tl = chunk_cols(n)
                if n % 2 == 0:
                    for g in range(2):
                        wait_read(pe, ("XT", t, LEVELS - 1, g))
                o = begin(("rhs", n))
                if n > 0:
                    wait_read(pe, ("S", n - 1))
                for cc in range(CT):
                    if n > 0:
                        mm(o[tl, cc * P:(cc + 1) * P], lhsT=ar[:, cc, 0, tc], rhs=state[:, cc, :], start=True, stop=True,
                           skip_group_check=True)
                    for h in (2 * cc, 2 * cc + 1):
                        ins = mm(o[tl, h * HD:(h + 1) * HD], lhsT=gram[:, h, 2, tl], rhs=vtok[:, t, h * HD:(h + 1) * HD],
                                 start=(n == 0), stop=True, skip_group_check=True)
                end(ins, ("rhs", n))

            def chunk_u(n):
                t, tc, tl = chunk_cols(n)
                o = begin(("U", n))
                wait_read(pe, ("rhs", n))
                for h in range(HEADS):
                    ins = mm(o[tl, h * HD:(h + 1) * HD], lhsT=XT[:, h, tl], rhs=rhs_sb[:, h * HD:(h + 1) * HD],
                             start=True, stop=True)
                end(ins, ("U", n))

            def chunk_y(n):
                t, tc, tl = chunk_cols(n)
                o = begin(("Y", n))
                for cc in range(CT):
                    if n > 0:
                        mm(o[tl, cc * P:(cc + 1) * P], lhsT=ar[:, cc, 1, tc], rhs=state[:, cc, :], start=True, stop=True,
                           skip_group_check=True)
                    for h in (2 * cc, 2 * cc + 1):
                        hs = slice(h * HD, (h + 1) * HD)
                        mm(o[tl, hs], lhsT=gram[:, h, 3, tl], rhs=vtok[:, t, hs], start=(n == 0), stop=False,
                           skip_group_check=True)
                        if h == 0:
                            wait_read(pe, ("U", n))
                        ins = mm(o[tl, hs], lhsT=gram[:, h, 1, tl], rhs=U[:, hs], start=False, stop=True,
                                 skip_group_check=True)
                end(ins, ("Y", n))
                if n < NCHUNK - 1:
                    o = begin(("S", n))
                    for cc in range(CT):
                        cols = slice(cc * P, (cc + 1) * P)
                        mm(o[:, cols], lhsT=btok[tl, t, cols], rhs=U[tl, cols], start=True, stop=False)
                        ins = mm(o[:, cols], lhsT=ktok[tl, t, cols], rhs=vtok[tl, t, cols], start=False, stop=True)
                    end(ins, ("S", n))

            def chunk_out(t):
                pe.wait_ge(sg["y_ready"], t + 1)
                transposes(("yt", t), [ytok[:, t, i * P:(i + 1) * P] for i in range(CT)])

            ys = (y_mem, y_att, y_rwkv)
            count = {"gate": 0, "up": 0}

            def gate():
                channels("gate", count["gate"] + 1, nT, count["gate"])
                count["gate"] += 1

            def up():
                u = count["up"]
                count["up"] += 1
                if u == 0:
                    wait_read(pe, ("mpv", 0))
                    wait_read(pe, ("mpv", 1))
                if u == 4:
                    for hp in range(4):
                        wait_read(pe, ("apv", hp))
                if u == 8:
                    wait_read(pe, ("yt", 0))
                    wait_read(pe, ("yt", 1))
                o, w = begin_unit("up", u, u // 2)
                for m in range(2):
                    for k in range(4):
                        ins = mm(o[:, m, :], lhsT=w[:, 4 * (u % 2) + k, m * P:(m + 1) * P], rhs=ys[u // 4][:, k, :],
                                 start=(k == 0), stop=(k == 3))
                ins.then_inc(proj_full, 1)

            stages = {"sumsq": sumsq, "spread": spread, "rope": rope, "gram": gram_matrices, "inverse": inverse, "rhs": chunk_rhs,
                      "u": chunk_u, "y": chunk_y, "out": chunk_out, "score": attention_scores,
                      "pair": attention_pair, "gate": gate, "up": up}
            for step in SCHEDULE:
                if step[0] in stages:
                    stages[step[0]](*step[1:])
            while count["up"] < 12:
                up()
            pe.wait_ge(sg["merged_ok"], 4)
            for i in range(5):
                if i < 4:
                    tokens("out", i + 1, merged, i)
                if i > 0:
                    wait_unit_read(pe, "out", i - 1)
                    transposes(("ht", i - 1), [h_tok[:, t, 256 * i - 256 + P * m:256 * i - 256 + P * m + P]
                                               for m in range(2) for t in range(TILES)])
            for i in range(4):
                wait_read(pe, ("ht", i))
            for j in list(JOB)[-BANKS:]:
                wait_read(pe, j)
            def add_group(t, n, g):
                pe.wait_ge(sg["diag_ok"], n * HEAD_GROUPS + (g + 1))
                for s in range(GROUP * g, GROUP * g + GROUP):
                    for d in range(2):
                        ins = mm(sum_bank(t, d), lhsT=diag[:, s % (2 * GROUP), :],
                                 rhs=slot[s % SLOTS][:, D + 512 * d:D + 512 * d + 512],
                                 start=False, stop=True, skip_group_check=True)
                ins.then_inc(sg["group_free"], 1)

            todo = [(n, g) for n in range(2) for g in range(HEAD_GROUPS)]

            def add_groups(n):
                for _ in range(n):
                    add_group(0, *todo.pop(0))

            for i in range(PEER_HEADS):
                channels("peer_q", i + 1, hT, i, lambda: add_groups(QUERY_GROUPS[i][0]))
                if i == 0:
                    key_scores(pe, mm, 0)
                    for t in range(TILES):
                        for d in range(2):
                            mm(sum_bank(t, d), lhsT=ident, rhs=h_tok[:, t, 512 * d:512 * d + 512],
                               start=True, stop=True, skip_group_check=True)
                add_groups(QUERY_GROUPS[i][1])
                if i > 0:
                    key_scores(pe, mm, i)
            for n, g in todo:
                add_group(0, n, g)
            for t in range(TILES):
                with pe.Fori(1 - t, PEER_HEADS // 2) as i:
                    for par in range(2):
                        for g in range(HEAD_GROUPS):
                            add_group(t, i * 2 + (PEER_HEADS * t + par), g)

        @block.scalar
        def _(act):
            st = Steps(act, act_step)
            A = nc.scalar.activation

            def squares(x, src):
                act.wait_ge(tokens_in[x], 16)
                for i in range(2):
                    A(in_sq[x][:, 4 * i:4 * i + 4, :], src[:, 4 * i:4 * i + 4, :], ACT.Square).then_inc(sg["ssq"], 1)

            def root(x, n):
                wait_job(act, (x + "_ss",))
                job_read(A(stat[x], bank((x + "_ss",))[:, 0:TILES * SUMS[x]], ACT.Sqrt, scale=1.0 / n, bias=eps_col),
                         (x + "_ss",))

            squares("x", nT)
            squares("mem", mT)
            act.wait_ge(sg["pads"], 1)
            root("x", D)
            wait_job(act, ("x_rn", 0))
            job_read(nc.scalar.copy(x_rn, bank(("x_rn", 0))[:, 0:S]), ("x_rn", 0))
            root("mem", D)
            for i in range(2):
                wait_unit(act, "mem_k", i)
                nc.scalar.copy(kmT[:, 2 * i:2 * i + 2, :], halves(ubank("mem_k", i)))
                unit_read(A(mem_sq["mk"][:, 2 * i:2 * i + 2, :], halves(ubank("mem_k", i)), ACT.Square), "mem_k", i)
            act.wait_ge(sg["mixed_ok"], 7)
            st(A(w_tanh, mixed[0:64, 12, :], ACT.Tanh)).wait()
            A(g_sig, mixed[:, 13, :], ACT.Sigmoid).then_inc(sg["lora_in"], 1)
            act.wait_ge(sg["kk_ok"], 1)
            A(knorm, kk, ACT.Square).then_inc(sg["kk2_ok"], 1)
            root("mk", P)
            for j, b, dst in (("wl", "w0", sgw), ("al", "a0", a_gate)):
                for i in range(2):
                    wait_job(act, (j, i))
                    for m in range(2):
                        ins = A(dst[:, 2 * i + m, :], bank((j, i))[:, m * S:(m + 1) * S], ACT.Sigmoid,
                                bias=v(b, 2 * i + m))
                    job_read(ins, (j, i))
            for i in range(2):
                wait_unit(act, "mem_v", i)
                unit_read(nc.scalar.copy(vm[:, :, 256 * i:256 * i + 256], halves(ubank("mem_v", i))), "mem_v", i)
            act.wait_ge(sg["lex_ok"], 1)
            st(A(p_inv, cum, ACT.Exp, scale=DECAY)).wait()
            st(A(cum, cum, ACT.Exp, scale=-DECAY))
            A(p_ex, p_ex, ACT.Exp, scale=-DECAY).then_inc(sg["decay_ok"], 1)
            wait_read(act, ("kn_ss",))
            A(stat["kn"], stat["kn"], ACT.Sqrt).then_inc(sg["kroot"], 1)
            for t in range(TILES):
                wait_job(act, ("vt", t))
                job_read(nc.scalar.copy(vtok[:, t, :], bank(("vt", t))), ("vt", t))
            for i in range(2):
                wait_unit(act, "mem_q", i)
                nc.scalar.copy(mqT[:, 2 * i:2 * i + 2, :], halves(ubank("mem_q", i)))
                unit_read(A(mem_sq["mq"][:, 2 * i:2 * i + 2, :], halves(ubank("mem_q", i)), ACT.Square), "mem_q", i)
            root("mq", P)
            act.wait_ge(sg["trig_arg"], 2)
            A(trig[:, :, :], trig[:, :, :], ACT.Sin).then_inc(sg["trig_ok"], 1)
            wait_unit(act, "idx_q", 0)
            unit_read(nc.scalar.copy(iqT, halves(ubank("idx_q", 0))), "idx_q", 0)
            wait_unit(act, "idx_k", 0)
            st(nc.scalar.copy(ikT, ubank("idx_k", 0)[:, 0:S]))
            unit_read(nc.scalar.mul(sm(IW, 8), ubank("idx_k", 0)[:, S:S + 8], 1.0 / 16), "idx_k", 0)
            for i in range(2):
                wait_unit(act, "v", i)
                unit_read(nc.scalar.copy(v_tok[:, :, 256 * i:256 * i + 256], halves(ubank("v", i))), "v", i)

            def sigmoid_gate(name, i):
                wait_unit(act, name, i)
                n = i + (N_GATE0 if name == "gate" else 0)
                for m in range(2):
                    ins = A(gates[:, 2 * n + m, :], ubank(name, i)[:, m * S:(m + 1) * S], ACT.Sigmoid,
                            bias=v("gate_bias", 2 * n + m))
                unit_read(ins, name, i)

            sigmoid_gate("gate0", 0)
            for t in range(TILES):
                for hp in range(2):
                    wait_job(act, ("ms", t, hp))
                    act.wait_ge(sg["mmax"], 2 * t + hp + 1)
                    for m in range(2):
                        hh = 2 * hp + m
                        ins = A(mprob[:, t, hh, :], bank(("ms", t, hp))[:, m * S:(m + 1) * S], ACT.Exp,
                                scale=float(P) ** -0.5, bias=sm(NMX + 4 * t + hh), accum_out=sm(SU + 4 * t + hh))
                    job_read(ins, ("ms", t, hp))

            for t in range(TILES):
                for i in range(2):
                    wait_job(act, ("il", t, i))
                    if 2 * t + i > 0:
                        act.wait_ge(sg["relu_used"], 2 * t + i)
                    job_read(A(idx_relu, halves(bank(("il", t, i))), ACT.Relu), ("il", t, i))
            for j, dst in (("bt", btok), ("kt", ktok)):
                for t in range(TILES):
                    wait_job(act, (j, t))
                    job_read(nc.scalar.copy(dst[:, t, :], bank((j, t))), (j, t))
                if j == "bt":
                    for i in range(1, N_GATE0):
                        sigmoid_gate("gate0", i)
            for t in range(TILES):
                wait_job(act, ("bonus", t))
                job_read(nc.scalar.copy(sm(BON + 8 * t, 8), bank(("bonus", t))[:, 0:8]), ("bonus", t))
            for t in range(TILES):
                wait_job(act, ("g", t))
                job_read(nc.scalar.copy(gtok[:, t, :], bank(("g", t))), ("g", t))

            def raw_and_square(x):
                for i in range(2):
                    wait_unit(act, x, i)
                    nc.scalar.copy(rope_raw[x][:, 2 * i:2 * i + 2, :], halves(ubank(x, i)))
                    unit_read(A(rope_sq[x][:, 2 * i:2 * i + 2, :], halves(ubank(x, i)), ACT.Square), x, i)

            raw_and_square("q")
            for t in range(TILES):
                for hp in range(2):
                    wait_job(act, ("mpt", t, hp))
                    job_read(nc.scalar.copy(mprobT[:, t, 2 * hp:2 * hp + 2, :, :].rearrange("p a b c -> p (a b c)"),
                                            bank(("mpt", t, hp))), ("mpt", t, hp))
            for hp in range(2):
                wait_job(act, ("mpv", hp))
                job_read(nc.scalar.copy(y_mem[:, 2 * hp:2 * hp + 2, :], halves(bank(("mpv", hp)))), ("mpv", hp))
            raw_and_square("k")

            def sumsq(x):
                root(x, HD)

            def attention_exp(hp):
                act.wait_ge(sg["amax"], hp + 1)
                for m in range(2):
                    for t in range(TILES):
                        ins = A(prob[:, 2 * (hp % 2) + t, m, :], prob[:, 2 * (hp % 2) + t, m, :], ACT.Exp,
                                bias=sm(NMX + 4 * (hp % 2) + 2 * t + m), accum_out=sm(SU + 4 * (hp % 2) + 2 * t + m))
                ins.then_inc(sg["aexp"], 1)

            def inverse(t, l):
                for g in range(2):
                    if l > 0:
                        wait_job(act, ("A", t, l, g))
                        job_read(nc.scalar.copy(A1[:, 4 * g:4 * g + 4, :].rearrange("p a b -> p (a b)"),
                                                bank(("A", t, l, g))), ("A", t, l, g))

            def chunk_copy(job, n, dst):
                tl = slice(CHUNK * (n % 2), CHUNK * (n % 2) + CHUNK)
                if (job, n) == ("rhs", 0):
                    act.wait_ge(sg["cleared"], 1)
                wait_job(act, (job, n))
                job_read(nc.scalar.copy(dst[tl, :], bank((job, n))[tl, :]), (job, n))

            def norm(t):
                act.wait_ge(sg["gn_sq"], t + 1)
                A(sm(GN + 8, 8), sm(GN + 8, 8), ACT.Sqrt, scale=1.0 / HD, bias=gn_eps_col).then_inc(sg["gn_root"], 1)

            def chunk_out(t):
                wait_job(act, ("yt", t))
                job_read(nc.scalar.copy(y_rwkv[:, :, t * P:(t + 1) * P],
                                        bank(("yt", t)).rearrange("p (a b) -> p a b", a=CT)), ("yt", t))
                if t == TILES - 1:
                    act.dma_start(x_again, t_in["x"].rearrange("(t p) d -> p t d", p=P)).then_inc(late_in, 16)
                    act.dma_start(gain_row, t_in["ffn_gain"].partition_broadcast(P)).then_inc(late_in, 16)
                    act.dma_start(keysT, t_in["keysT"]).then_inc(late_in, 16)

            gate_next = [0]

            def gate():
                sigmoid_gate("gate", gate_next[0])
                gate_next[0] += 1

            stages = {"sumsq": sumsq, "inverse": inverse, "gate": gate, "norm": norm, "out": chunk_out,
                      "rhs": lambda n: chunk_copy("rhs", n, rhs_sb), "u": lambda n: chunk_copy("U", n, U),
                      "y": lambda n: chunk_copy("Y", n, ytok[:, n // 2, :]),
                      "exp": attention_exp}
            for step in SCHEDULE:
                if step[0] in stages:
                    stages[step[0]](*step[1:])
            for i in range(4):
                wait_job(act, ("ht", i))
                for m in range(2):
                    ins = A(hT[:, 2 * i + m, :], bank(("ht", i))[:, m * S:(m + 1) * S], ACT.Copy,
                            scale=v("ffn_gain", 2 * i + m))
                job_read(ins, ("ht", i))
            for t in range(TILES):
                act.wait_ge(sg["h_ssq"], t + 1)
                A(sm(HS + 2 + t), sm(HS + t), ACT.Sqrt, scale=1.0 / D, bias=eps_col).then_inc(sg["h_root"], 1)
            sc4 = scores[:, 0:PEER_HEADS * TILES * 256].rearrange("p (t h k) -> p t h k", t=TILES, h=PEER_HEADS)

            def copy_scores(h):
                act.wait_ge(sg["ps_full"], h + 1)
                if h == 0:
                    act.wait_ge(sg["h_rstd"], TILES)
                for t in range(TILES):
                    ins = A(sc4[:, t, h, :], score_bank(h)[:, t * S:(t + 1) * S], ACT.Copy, scale=sm(HS + 4 + t))
                ins.then_inc(sg["ps_free"], 1)

            def stage_scores(par, n):
                start = n * 256
                nc.scalar.copy(stage[:, par].rearrange("p a b -> p (a b)"), scores[:, bass.ds(start, 256)]
                               ).then_inc(sg["stage_ok"], 1)

            def soften(par, n):
                act.wait_ge(sg["gate_in"], n + 1)
                A(gate_e[:, par, :], top[:, par, :], ACT.Exp, bias=gstat[:, par, 0:1],
                  accum_out=gstat[:, par, 1:2]).then_inc(sg["gsum"], 1)

            def gelu(par, n, g):
                if g == 3:
                    act.wait_ge(sg["stage_used"], n + 1)
                    stage_scores(par, n + 2)
                act.wait_ge(sg["dots"], n * HEAD_GROUPS + (g + 1))
                A(act_h[:, par, GROUP * g:GROUP * g + GROUP], hid[:, par, GROUP * g:GROUP * g + GROUP],
                  ACT.Gelu).then_inc(sg["gelu_ok"], 1)
                if g == 1:
                    soften(1 - par, n + 1)

            todo = [(n, g) for n in range(2) for g in range(HEAD_GROUPS)]

            def gelus(m):
                for _ in range(m):
                    n, g = todo.pop(0)
                    gelu(n, n, g)

            for h in range(PEER_HEADS):
                gelus(QUERY_GROUPS[h][0])
                wait_unit(act, "peer_q", h)
                if h >= 2:
                    act.wait_ge(sg["ps_full"], h - 1)
                unit_read(nc.scalar.copy(qp[h % 2], halves(ubank("peer_q", h))), "peer_q", h)
                gelus(QUERY_GROUPS[h][1])
                copy_scores(h)
                act.wait_ge(sg["ps_free"], h + 1)
                if h < 2:
                    stage_scores(h, h)
                if h == 0:
                    soften(0, 0)
            for n, g in todo:
                gelu(n, n, g)
            for t in range(TILES):
                with act.Fori(1 - t, PEER_HEADS // 2) as i:
                    for par in range(2):
                        n = i * 2 + (PEER_HEADS * t + par)
                        for g in range(HEAD_GROUPS):
                            gelu(par, n, g)
                act.wait_ge(sg["group_free"], RING_GROUPS + PEER_HEADS * HEAD_GROUPS * (t + 1))
                if t > 0:
                    act.wait_ge(sg["stored"], 16 * t)
                for d in range(2):
                    nc.scalar.copy(o_sb[:, 512 * d:512 * d + 512], sum_bank(t, d)).then_inc(sg["o_sb_ok"], 1)

        @block.vector
        def _(dve):
            st = Steps(dve, dve_step)
            V = nc.vector

            def inverse_roots(x):
                if x in wide:
                    st(V.reciprocal(stat[x], stat[x])).wait()
                    V.tensor_copy(wide[x].rearrange("p t (h i) -> p (t h) i", i=HD),
                                  stat[x].unsqueeze(2).to_broadcast([P, TILES * HEADS, HD])).then_inc(rms_ok[x], 1)
                else:
                    V.reciprocal(stat[x], stat[x]).then_inc(rms_ok[x], 1)

            dve.wait_ge(vec_in, 16)
            for i in range(2):
                dve.wait_ge(sg["ssq"], i + 1)
                for k in range(4 * i, 4 * i + 4):
                    ins = V.tensor_scalar(nT[:, k, :], nT[:, k, :], v("mix_gain", k), None, ALU.mult)
                ins.then_inc(sg["x_gained"], 1)
            wait_read(dve, ("x_ss",))
            inverse_roots("x")
            dve.wait_ge(sg["mix_pad"], 1)
            wait_read(dve, ("x_rn", 0))
            for i in range(7):
                sl = slice(2 * i, 2 * i + 2)
                wait_unit(dve, "rwkv", i)
                unit_read(V.tensor_tensor(pT[:, sl, 1:S + 1], halves(ubank("rwkv", i)),
                                          x_rn.unsqueeze(1).to_broadcast([P, 2, S]), ALU.mult), "rwkv", i)
                wait_unit_read(dve, "rwkv", i)
                st(V.tensor_tensor(mixed[:, sl, :], pT[:, sl, 0:S], pT[:, sl, 1:S + 1], ALU.subtract)).wait()
                for m in range(2):
                    ins = V.scalar_tensor_tensor(mixed[:, 2 * i + m, :], mixed[:, 2 * i + m, :], v("mu", 2 * i + m),
                                                 pT[:, 2 * i + m, 1:S + 1], ALU.mult, ALU.add)
                ins.then_inc(sg["mixed_ok"], 1)
                if i == 2:
                    wait_read(dve, ("mem_ss",))
                    inverse_roots("mem")
                if i == 4:
                    job = spread_jobs("mem")[0]
                    wait_job(dve, job)
                    for k in range(KT):
                        ins = V.scalar_tensor_tensor(mT[:, k, :], mT[:, k, :], v("mem_gain", k), bank(job)[:, 0:S],
                                                     ALU.mult, ALU.mult)
                    job_read(ins, job)
            V.tensor_tensor(nT, nT, x_rn.unsqueeze(1).to_broadcast([P, KT, S]), ALU.mult).then_inc(sg["n_ok"], 1)
            dve.wait_ge(sg["mixed_ok"], 7)
            r_, k_ = mixed[:, 0:4, :], mixed[:, 4:8, :]
            for i in range(CT):
                V.tensor_scalar(kk[:, i, :], k_[:, i, :], v("k_k", i), None, ALU.mult)
            V.tensor_scalar(sm(OMKA, 4), v("k_a", 0, 4), -1.0, 1.0, ALU.mult, ALU.add).then_inc(sg["kk_ok"], 1)
            dve.wait_ge(sg["kk_ok"], 1)
            st(V.tensor_copy(trig[:, 0, :], pos_i[:, :])).wait()
            st(V.tensor_scalar(trig[:, 1, :], trig[:, 0, :], c("inv_freq"), None, ALU.mult)).wait()
            ang, turns, arg = trig[:, 1, :], work[:, 0, :], work[:, 1, :]
            MAGIC = 12582912.0
            C1, C2 = 6.28125, 0.0019340515136718750
            C3 = float(2 * np.pi - C1 - C2)
            for which, shift in ((0, 0.25), (1, 0.0)):
                st(V.tensor_scalar(turns, ang, float(1 / (2 * np.pi)), shift, ALU.mult, ALU.add)).wait()
                st(V.tensor_scalar(turns, turns, MAGIC, None, ALU.add)).wait()
                st(V.tensor_scalar(turns, turns, MAGIC, None, ALU.subtract)).wait()
                st(V.scalar_tensor_tensor(arg, turns, -C1, ang, ALU.mult, ALU.add)).wait()
                st(V.scalar_tensor_tensor(arg, turns, -C2, arg, ALU.mult, ALU.add)).wait()
                st(V.scalar_tensor_tensor(arg, turns, -C3, arg, ALU.mult, ALU.add)).wait()
                st(V.tensor_scalar(arg, arg, float(np.pi / 2) if which == 0 else 0.0, None, ALU.add)).wait()
                V.tensor_scalar(trig[:, which, :], arg, 3.1415925, -3.1415925, ALU.min, ALU.max).then_inc(
                    sg["trig_arg"], 1)
            wait_read(dve, ("wl", 0))
            wait_read(dve, ("wl", 1))
            for i in range(CT):
                st(V.tensor_tensor_scan(cum[:, i, :], reset, sgw[:, i, :], 0.0, ALU.mult, ALU.add))
            st.wait()
            V.tensor_tensor(p_ex, cum, sgw, ALU.subtract).then_inc(sg["lex_ok"], 1)
            wait_job(dve, ("kn_ss",))
            job_read(V.tensor_scalar(stat["kn"], bank(("kn_ss",))[:, 0:TILES * SUMS["kn"]], 1e-24, None, ALU.max),
                     ("kn_ss",))
            wait_read(dve, ("al", 0))
            wait_read(dve, ("al", 1))
            for i in range(CT):
                st(V.tensor_scalar(kmod[:, i, :], a_gate[:, i, :], v("k_a", i), sm(OMKA + i), ALU.mult, ALU.add))
            st.wait()
            st(V.tensor_tensor(kmod, kmod, k_, ALU.mult))
            dve.wait_ge(sg["kroot"], 1)
            inverse_roots("kn")
            for i, job in enumerate(spread_jobs("kn")):
                wait_job(dve, job)
                job_read(V.tensor_tensor(kk[:, 2 * i:2 * i + 2, :], kk[:, 2 * i:2 * i + 2, :], halves(bank(job)),
                                         ALU.mult), job)
            for job in spread_jobs("kn"):
                wait_read(dve, job)
            dve.wait_ge(sg["decay_ok"], 1)
            st(V.scalar_tensor_tensor(ar[:, :, 0, :], kk, -1.0, p_ex, ALU.mult, ALU.mult))
            st(V.tensor_tensor(ar[:, :, 1, :], r_, cum, ALU.mult))
            st(V.tensor_tensor(kk, kk, a_gate, ALU.mult)).wait()
            st(V.tensor_tensor(bb, kk, p_inv, ALU.mult))
            st(V.tensor_tensor(kb, kmod, p_inv, ALU.mult)).wait()
            p_end = cum.rearrange("p c (n k) -> p (c n) k", k=CHUNK)[:, :, CHUNK - 1:CHUNK]
            for dst, src in ((b_end, bb), (k_end, kb)):
                V.tensor_tensor(dst.rearrange("p c (n k) -> p (c n) k", k=CHUNK),
                                src.rearrange("p c (n k) -> p (c n) k", k=CHUNK),
                                p_end.to_broadcast([P, CT * NCHUNK, CHUNK]), ALU.mult).then_inc(sg["ends_ok"], 1)
            for i in range(CT):
                ins = V.scalar_tensor_tensor(rkk[:, i, :], r_[:, i, :], v("r_k", i), kmod[:, i, :], ALU.mult, ALU.mult)
                if i < CT - 1:
                    st(ins)
            ins.then_inc(sg["ends_ok"], 1)
            V.tensor_copy(pend, p_end.rearrange("p a b -> p (a b)")).then_inc(sg["tilde_ok"], 1)
            for x, dst in (("mk", kmT), ("mq", mqT)):
                wait_read(dve, (x + "_ss",))
                inverse_roots(x)
            for x, dst in (("mk", kmT), ("mq", mqT)):
                for i, job in enumerate(spread_jobs(x)):
                    wait_job(dve, job)
                    job_read(V.scalar_tensor_tensor(dst[:, 2 * i:2 * i + 2, :], dst[:, 2 * i:2 * i + 2, :],
                                                    v(x + "_gain"), halves(bank(job)), ALU.mult, ALU.mult), job)

            dve.wait_ge(sg["trig_ok"], 1)
            wait_job(dve, ("iqrot", 0))
            cosb = trig[:, 0:1, :].to_broadcast([P, 2, S])
            sinb = trig[:, 1:2, :].to_broadcast([P, 2, S])
            st(V.tensor_tensor(iqT, iqT, cosb, ALU.mult))
            st(V.tensor_tensor(score, halves(bank(("iqrot", 0))), sinb, ALU.mult)).wait()
            job_read(V.tensor_tensor(iqT, iqT, score, ALU.add), ("iqrot", 0))
            wait_job(dve, ("ikrot", 0))
            st(V.tensor_tensor(ikT, ikT, trig[:, 0, :], ALU.mult))
            st(V.tensor_tensor(work[:, 0, :], bank(("ikrot", 0))[:, 0:S], trig[:, 1, :], ALU.mult)).wait()
            job_read(V.tensor_tensor(ikT, ikT, work[:, 0, :], ALU.add), ("ikrot", 0))
            wait_read(dve, ("ikrot", 0))
            wait_read(dve, ("iqrot", 0))
            def row_max(t, hp):
                wait_job(dve, ("ms", t, hp))
                st(V.tensor_reduce(sm(MX + 4 * t + 2 * hp, 2), halves(bank(("ms", t, hp))), AX, ALU.max)).wait()
                V.tensor_scalar(sm(NMX + 4 * t + 2 * hp, 2), sm(MX + 4 * t + 2 * hp, 2), -float(P) ** -0.5, None,
                                ALU.mult).then_inc(sg["mmax"], 1)

            for t in range(TILES):
                for hp in range(2):
                    row_max(t, hp)
            for t in range(TILES):
                for i in range(2):
                    wait_read(dve, ("il", t, i))
                    for m in range(2):
                        hh = 2 * m + i
                        iw = sm(IW + 4 * t + hh)
                        if i == 0 and m == 0:
                            st(V.tensor_scalar(score[:, t, :], idx_relu[:, m, :], iw, None, ALU.mult)).wait()
                        else:
                            ins = V.scalar_tensor_tensor(score[:, t, :], idx_relu[:, m, :], iw, score[:, t, :],
                                                         ALU.mult, ALU.add)
                            if m == 0:
                                st(ins).wait()
                    ins.then_inc(sg["relu_used"], 1)
                    dve.wait_ge(sg["relu_used"], 2 * t + i + 1)
                near = slice(t * P, (t + 1) * P)
                st(V.tensor_tensor(score[:, t, near], score[:, t, near], c("causal"), ALU.add)).wait()

            for t in range(TILES):
                wait_read(dve, ("ms", t, 0))
                wait_read(dve, ("ms", t, 1))
                st(V.reciprocal(sm(RS, 4), sm(SU + 4 * t, 4))).wait()
                ins = V.tensor_tensor(mprob[:, t], mprob[:, t], sm(RS, 4).unsqueeze(2).to_broadcast([P, 4, S]), ALU.mult)
                ins.then_inc(sg["mscaled"], 1)
                dve.wait_ge(sg["mscaled"], t + 1)
            def top_keys(t):
                reach = slice(0, (t + 1) * P)
                for r in range(N_SEL // 8):
                    src = score[:, t, reach] if r == 0 else work[:, t, reach]
                    st(V.max(sm(MX, 8), src)).wait()
                    st(V.match_replace(work[:, t, reach], sm(MX, 8), src, TAKEN)).wait()
                st(V.tensor_scalar(work[:, t, reach], work[:, t, reach], TAKEN / 2, OFF, ALU.is_gt, ALU.mult))
                st(V.tensor_scalar(score[:, t, reach], score[:, t, reach], OFF / 2, OFF, ALU.is_lt, ALU.mult)).wait()
                st(V.tensor_tensor(bias[:, t, reach], work[:, t, reach], score[:, t, reach], ALU.add)).wait()
                if t == 0:
                    st(V.memset(bias[:, 0, P:S], OFF)).wait()

            qk_dst = {"q": qT, "k": kT}

            def normed(x):
                wait_read(dve, (x + "_ss",))
                inverse_roots(x)

            def scaled(x):
                for i, job in enumerate(spread_jobs(x)):
                    wait_job(dve, job)
                    job_read(V.scalar_tensor_tensor(rope_sq[x][:, 2 * i:2 * i + 2, :], rope_raw[x][:, 2 * i:2 * i + 2, :],
                                                    v(x + "_gain"), halves(bank(job)), ALU.mult, ALU.mult), job)
                for job in spread_jobs(x):
                    wait_read(dve, job)
                st(V.tensor_tensor(qk_dst[x], rope_sq[x], trig[:, 0:1, :].to_broadcast([P, CT, S]), ALU.mult))

            def rope(x):
                for i in range(2):
                    wait_job(dve, (x + "rot", i))
                    job_read(V.tensor_tensor(rope_raw[x][:, 2 * i:2 * i + 2, :], halves(bank((x + "rot", i))), sinb,
                                             ALU.mult), (x + "rot", i))
                wait_read(dve, (x + "rot", 0))
                wait_read(dve, (x + "rot", 1))
                st.wait()
                V.tensor_tensor(qk_dst[x], qk_dst[x], rope_raw[x], ALU.add).then_inc(sg["rope_ok"], 1)

            def attention_max(hp):
                if hp > 1:
                    wait_job(dve, ("apt", hp - 2, 1))
                for m in range(2):
                    wait_job(dve, ("as", hp, m))
                    for t in range(TILES):
                        p = prob[:, 2 * (hp % 2) + t, m, :]
                        ins = V.scalar_tensor_tensor(p, bank(("as", hp, m))[:, t * S:(t + 1) * S], HD ** -0.5,
                                                     bias[:, t, :], ALU.mult, ALU.add)
                    job_read(ins, ("as", hp, m))
                    wait_read(dve, ("as", hp, m))
                a = 4 * (hp % 2)
                st(V.tensor_reduce(sm(MX + a, 4), prob[:, 2 * (hp % 2):2 * (hp % 2) + 2, :, :].rearrange(
                    "p a b c -> p (a b) c"), AX, ALU.max)).wait()
                V.tensor_scalar(sm(NMX + a, 4), sm(MX + a, 4), -1.0, None, ALU.mult).then_inc(sg["amax"], 1)

            def attention_scale(hp):
                a = 4 * (hp % 2)
                dve.wait_ge(sg["aexp"], hp + 1)
                st(V.reciprocal(sm(RS + a, 4), sm(SU + a, 4))).wait()
                pr = prob[:, 2 * (hp % 2):2 * (hp % 2) + 2, :, :].rearrange("p a b c -> p (a b) c")
                V.tensor_tensor(pr, pr, sm(RS + a, 4).unsqueeze(2).to_broadcast([P, 4, S]), ALU.mult
                                ).then_inc(sg["ascaled"], 1)

            def attention_out(hp):
                for i in range(2):
                    wait_job(dve, ("apt", hp, i))
                    job_read(V.tensor_copy(probT[:, 2 * (hp % 2) + i].rearrange("p a b c -> p (a b c)"),
                                           bank(("apt", hp, i))), ("apt", hp, i))
                wait_job(dve, ("apv", hp))
                o = halves(bank(("apv", hp)))
                st(V.tensor_copy(y_att[0:64, hp, :], o[0:64, 0, :]))
                job_read(V.tensor_copy(y_att[64:128, hp, :], o[64:128, 1, :]), ("apv", hp))

            def attention_pair(hp):
                attention_out(hp)
                if hp < 2:
                    attention_max(hp + 2)
                if hp < 3:
                    attention_scale(hp + 1)

            def attention_score(hp):
                attention_max(hp)
                if hp == 1:
                    attention_scale(0)

            def gram_matrices(t, g):
                for h in range(4 * g, 4 * g + 4):
                    wait_job(dve, ("gram", t, h))
                    job_read(V.tensor_tensor(gram[:, h, :, :].rearrange("p a b -> p (a b)"), bank(("gram", t, h)),
                                             c("gram_mask"), ALU.mult), ("gram", t, h))

            def inverse(t, l):
                for name, dst in (("A", X), ("X", X), ("XT", XT)):
                    if (name, t, l, 0) not in JOB or (name == "A" and l > 0):
                        continue
                    for g in range(2):
                        job = (name, t, l, g)
                        d = dst[:, 4 * g:4 * g + 4, :]
                        wait_job(dve, job)
                        old = ident.unsqueeze(1).to_broadcast([P, 4, P]) if l == 0 else d
                        job_read(V.tensor_tensor(d, old, bank(job).rearrange("p (a b) -> p a b", a=4), ALU.add), job)
                    for g in range(2):
                        wait_read(dve, (name, t, l, g))

            def chunk_rhs(n):
                if n == 0:
                    st(V.memset(U, 0.0))
                    st(V.memset(rhs_sb, 0.0))
                    V.memset(state, 0.0).then_inc(sg["cleared"], 1)
                    dve.wait_ge(sg["cleared"], 1)

            def chunk_state(n):
                if n == NCHUNK - 1:
                    return
                wait_job(dve, ("S", n))
                pe_n = pend.rearrange("p (c n) -> p c n", n=NCHUNK)[:, :, n:n + 1]
                for m in range(2):
                    r = slice(HD * m, HD * m + HD)
                    st(V.tensor_tensor(state[r, :, r], state[r, :, r], pe_n[r].to_broadcast([HD, CT, HD]), ALU.mult))
                st.wait()
                for m in range(2):
                    r = slice(HD * m, HD * m + HD)
                    ins = V.tensor_tensor(state[r, :, r], state[r, :, r],
                                          bank(("S", n)).rearrange("p (a b) -> p a b", a=CT)[r, :, r], ALU.add)
                    if m == 0:
                        st(ins)
                job_read(ins, ("S", n))
                wait_read(dve, ("S", n))

            def group_norm(t):
                wait_read(dve, ("Y", 2 * t))
                wait_read(dve, ("Y", 2 * t + 1))
                y3 = ytok[:, t, :].rearrange("p (h i) -> p h i", h=HEADS)
                g3 = gn_tmp.rearrange("p (h i) -> p h i", h=HEADS)
                v3 = vtok[:, t, :].rearrange("p (h i) -> p h i", h=HEADS)
                st(V.tensor_reduce(sm(GN, 8), y3, AX, ALU.add)).wait()
                st(V.tensor_scalar(sm(GN, 8), sm(GN, 8), 1.0 / HD, None, ALU.mult)).wait()
                st(V.tensor_tensor(y3, y3, sm(GN, 8).unsqueeze(2).to_broadcast([P, 8, HD]), ALU.subtract)).wait()
                st(V.tensor_tensor(g3, y3, y3, ALU.mult)).wait()
                V.tensor_reduce(sm(GN + 8, 8), g3, AX, ALU.add).then_inc(sg["gn_sq"], 1)
                dve.wait_ge(sg["gn_root"], t + 1)
                st(V.tensor_tensor(g3, v3, sm(BON + 8 * t, 8).unsqueeze(2).to_broadcast([P, 8, HD]), ALU.mult))
                st(V.reciprocal(sm(GN + 16, 8), sm(GN + 8, 8))).wait()
                st(V.tensor_tensor(y3, y3, sm(GN + 16, 8).unsqueeze(2).to_broadcast([P, 8, HD]), ALU.mult)).wait()
                st(V.tensor_tensor(ytok[:, t, :], ytok[:, t, :], rows[:, 0:W], ALU.mult)).wait()
                st(V.tensor_tensor(ytok[:, t, :], ytok[:, t, :], rows[:, W:2 * W], ALU.add)).wait()
                st(V.tensor_tensor(ytok[:, t, :], ytok[:, t, :], gn_tmp, ALU.add)).wait()
                V.tensor_tensor(ytok[:, t, :], ytok[:, t, :], gtok[:, t, :], ALU.mult).then_inc(sg["y_ready"], 1)
                dve.wait_ge(sg["y_ready"], t + 1)

            up_next = [0]

            def up():
                u = up_next[0]
                up_next[0] += 1
                br, grp = u // 4, u % 4
                gt = gates[:, 2 * u:2 * u + 2, :]
                m2 = merged[:, 2 * grp:2 * grp + 2, :]
                if grp == 0:
                    for i in (4 * br + 2, 4 * br + 3):
                        wait_unit_read(dve, "gate", i - N_GATE0)
                wait_unit(dve, "up", u)
                if br == 0:
                    unit_read(V.tensor_tensor(m2, halves(ubank("up", u)), gt, ALU.mult), "up", u)
                    wait_unit_read(dve, "up", u)
                else:
                    unit_read(V.tensor_tensor(tmp_up, halves(ubank("up", u)), gt, ALU.mult), "up", u)
                    wait_unit_read(dve, "up", u)
                    ins = V.tensor_tensor(m2, m2, tmp_up, ALU.add)
                    if br == 2:
                        ins.then_inc(sg["merged_ok"], 1)
                        dve.wait_ge(sg["merged_ok"], grp + 1)
                    else:
                        st(ins).wait()

            stages = {"sumsq": normed, "spread": scaled, "rope": rope, "top": top_keys, "gram": gram_matrices, "inverse": inverse,
                      "rhs": chunk_rhs, "y": chunk_state, "norm": group_norm, "score": attention_score,
                      "pair": attention_pair, "up": up}
            for step in SCHEDULE:
                if step[0] in stages:
                    stages[step[0]](*step[1:])
            while up_next[0] < 12:
                up()
            dve.wait_ge(late_in, 48)
            for i in range(4):
                wait_unit(dve, "out", i)
                cols = slice(256 * i, 256 * i + 256)
                unit_read(V.tensor_tensor(h_tok[:, :, cols], halves(ubank("out", i)), x_again[:, :, cols], ALU.add), "out", i)
            wait_unit_read(dve, "out", 2)
            wait_unit_read(dve, "out", 3)
            for t in range(TILES):
                V.tensor_tensor_reduce(xn_tok[:, t, :], h_tok[:, t, :], h_tok[:, t, :], 1.0, 0.0, ALU.mult, ALU.add,
                                       sm(HS + t)).then_inc(sg["h_ssq"], 1)
            for t in range(TILES):
                dve.wait_ge(sg["h_root"], t + 1)
                V.reciprocal(sm(HS + 4 + t), sm(HS + 2 + t)).then_inc(sg["h_rstd"], 1)
            dve.wait_ge(sg["h_rstd"], TILES)
            for t in range(TILES):
                V.scalar_tensor_tensor(xn_tok[:, t, :], h_tok[:, t, :], sm(HS + 4 + t), gain_row, ALU.mult,
                                       ALU.mult).then_inc(sg["xn_ok"], 1)

            n_choose = [0]

            def s(ins):
                ins.then_inc(sg["choose"], 1)
                n_choose[0] += 1

            def w():
                dve.wait_ge(sg["choose"], n_choose[0])

            def choose_halves(par, k):
                dve.sem_clear(sg["choose"])
                n_choose[0] = 0
                wait_alone(dve, sg["stage_ok"], k + 1)
                for half in range(2):
                    b8 = slice(8 * half, 8 * half + 8)
                    for side in range(2):
                        s(V.max(best[:, side, b8], stage[:, par, side, :]))
                    w()
                    for side in range(2):
                        s(V.max_index(best_i[:, side, b8], best[:, side, b8], stage[:, par, side, :]))
                    if half == 0:
                        w()
                        for side in range(2):
                            s(V.match_replace(stage[:, par, side, :], best[:, side, b8], stage[:, par, side, :], TAKEN))
                        w()
                w()
                V.tensor_copy(best_f[:, :, :], best_i[:, :, :]).then_inc(sg["stage_used"], 1)
                s(V.tensor_tensor(cand[:, :, :], best[:, 0, :].unsqueeze(2).to_broadcast([P, TOPK, TOPK]),
                                  best[:, 1, :].unsqueeze(1).to_broadcast([P, TOPK, TOPK]), ALU.add))
                w()
                dve.wait_ge(sg["stage_used"], k + 1)
                s(V.tensor_scalar(best_f[:, 0, :], best_f[:, 0, :], float(KEYS), None, ALU.mult))
                w()

            def choose_sums(par, k):
                cf = cand[:, :, :].rearrange("p a b -> p (a b)")
                s(V.max(top[:, par, 0:8], cf)); w()
                s(V.max_index(top_i[:, 0:8], top[:, par, 0:8], cf))
                s(V.tensor_scalar(gstat[:, par, 0:1], top[:, par, 0:1], -1.0, None, ALU.mult)); w()
                s(V.match_replace(cf, top[:, par, 0:8], cf, TAKEN)); w()
                s(V.max(top[:, par, 8:16], cf)); w()
                V.max_index(top_i[:, 8:16], top[:, par, 8:16], cf).then_inc(sg["gate_in"], 1)
                dve.wait_ge(sg["gate_in"], k + 1)

            def choose_experts(par, k):
                s(V.tensor_scalar(place_i[:, 0, :], top_i[:, :], 4, None, ALU.logical_shift_right))
                s(V.tensor_scalar(place_i[:, 1, :], top_i[:, :], 15, None, ALU.bitwise_and)); w()
                s(V.tensor_copy(place_f[:, :, :], place_i[:, :, :])); w()
                iota = c("iota").unsqueeze(1).to_broadcast([P, 2 * TOPK, TOPK])
                s(V.tensor_tensor(onehot[:, :, :], iota,
                                  place_f[:, :, :].rearrange("p a b -> p (a b)").unsqueeze(2).to_broadcast([P, 2 * TOPK, TOPK]),
                                  ALU.is_equal)); w()
                for side in range(2):
                    o = onehot[:, TOPK * side:TOPK * side + TOPK, :]
                    s(V.tensor_tensor(o, o, best_f[:, side:side + 1, :].to_broadcast([P, TOPK, TOPK]), ALU.mult))
                w()
                s(V.tensor_reduce(expert[:, :, :].rearrange("p a b -> p (a b)"), onehot[:, :, :], AX, ALU.add)); w()
                s(V.tensor_tensor(expert_f[:, :], expert[:, 0, :], expert[:, 1, :], ALU.add)); w()
                V.tensor_copy(expert_i[:, par, :], expert_f[:, :]).then_inc(sg["experts_ok"], 1)

            def choose_gates(par, k):
                dve.wait_ge(sg["gsum"], k + 1)
                s(V.reciprocal(gstat[:, par, 2:3], gstat[:, par, 1:2])); w()
                V.tensor_scalar(gate_e[:, par, :], gate_e[:, par, :], gstat[:, par, 2:3], None, ALU.mult).then_inc(
                    sg["gate_ok"], 1)

            def choose(par, k):
                for part_ in (choose_halves, choose_sums, choose_experts, choose_gates):
                    part_(par, k)

            def dots(par, n, g, t, between):
                for s_ in range(GROUP * g, GROUP * g + GROUP):
                    uses = n * 2 + s_ // SLOTS
                    dve.wait_ge(slot_in[s_ % SLOTS], uses * 16 + 16)
                    u = slot[s_ % SLOTS][:, 0:D]
                    ins = V.tensor_tensor_reduce(u, u, xn_tok[:, t, :], 1.0, 0.0, ALU.mult, ALU.add,
                                                 hid[:, par, s_:s_ + 1])
                    if s_ == GROUP * g:
                        between()
                ins.then_inc(sg["dots"], 1)

            def multiply(par, n, t):
                parts = {0: choose_halves, 1: choose_sums, 2: choose_experts, 3: choose_gates}
                dve.wait_ge(sg["gate_ok"], n + 1)
                for g in range(HEAD_GROUPS):
                    dots(par, n, g, t, lambda: diagonals(dve, V, n * HEAD_GROUPS + g, par, g - 1) if g > 0 else None)
                    if g in parts:
                        parts[g](1 - par, n + 1)
                diagonals(dve, V, n * HEAD_GROUPS + HEAD_GROUPS, par, HEAD_GROUPS - 1)

            dve.wait_ge(sg["xn_ok"], TILES)
            choose(0, 0)
            for n in range(2):
                multiply(n, n, 0)
            for t in range(TILES):
                with dve.Fori(1 - t, PEER_HEADS // 2) as i:
                    for par in range(2):
                        multiply(par, i * 2 + (PEER_HEADS * t + par), t)

        @block.gpsimd
        def _(pool):
            st = Steps(pool, pool_step)
            G_ = nc.gpsimd
            G_.memset(eps_col, EPS)
            G_.memset(gn_eps_col, GN_EPS).then_inc(sg["pads"], 1)
            G_.memset(pT[:, :, 0:1], 0.0)
            st(G_.memset(reset, 1.0)).wait()
            G_.memset(reset.rearrange("p (n k) -> p n k", k=CHUNK)[:, :, 0:1], 0.0).then_inc(sg["mix_pad"], 1)
            for t in range(TILES):
                wait_read(pool, ("gram", t, HEADS - 1))
                if t > 0:
                    wait_job(pool, ("U", 2 * t - 1))
                for l in range(LEVELS):
                    level = const[:, CONST["level"][0] + l * P:CONST["level"][0] + (l + 1) * P]
                    for g in range(2):
                        gs = slice(4 * g, 4 * g + 4)
                        if l > 0:
                            wait_job(pool, ("A", t, l - 1, g))
                        if l == 1:
                            pool.wait_ge(sg["xt0"], 2 * t + g + 1)
                        G_.tensor_tensor(LmT[:, gs, :], gram[:, gs, 0, :], level.unsqueeze(1).to_broadcast([P, 4, P]),
                                         ALU.mult).then_inc(sg["lm_ok"], 1)
                    if l == 0:
                        for g in range(2):
                            gs = slice(4 * g, 4 * g + 4)
                            pool.wait_ge(sg["lm_ok"], 2 * LEVELS * t + g + 1)
                            G_.tensor_tensor(XT[:, gs, :], LmT[:, gs, :], ident.unsqueeze(1).to_broadcast([P, 4, P]),
                                             ALU.add).then_inc(sg["xt0"], 1)
            pool.wait_ge(sg["experts_ok"], 1)
            pool.sem_inc(sg["group_free"], RING_GROUPS)
            with pool.Fori(0, PEER_HEADS * TILES // 2) as i:
                for par in range(2):
                    pool.wait_ge(sg["experts_ok"], i * 2 + (par + 1))
                    for s_ in range(TOPK):
                        if s_ % GROUP == 0:
                            wait_alone(pool, sg["group_free"], i * (2 * HEAD_GROUPS) + (HEAD_GROUPS * par + s_ // GROUP + 1))
                        G_.indirect_dma_start(slot[s_ % SLOTS], None, t_in["experts"],
                                              bass.IndirectOffsetOnAxis(ap=expert_i[:, par, s_:s_ + 1], axis=0)
                                              ).then_inc(slot_in[s_ % SLOTS], 16)


def _cols(w, a, n):
    w = w[:, a:a + n]
    return w.reshape(w.shape[0] // P, P, n // 256, 256).transpose(2, 1, 0, 3)


def _channel_major(x):
    return x.T.reshape(KT, P, S).transpose(1, 0, 2).reshape(P, KT * S)


def _vec(x):
    return np.asarray(x).reshape(-1, P).T


def kernel(**inputs):
    import concourse.bacc as bacc
    from concourse.bass_utils import run_bass_kernel_spmd

    a = {k: np.asarray(x) for k, x in inputs.items()}
    w_in = a["w_in"][0]
    pad = np.zeros((D, 124), np.float32)
    idx_k = np.concatenate([w_in[:, 1792:1856], w_in[:, 1792:1856], w_in[:, 1856:1860], pad], axis=1)
    w_up = a["w_up"][0][list(BRANCH_ORDER)].reshape(3, 4, P, 4, 256)
    gate = np.concatenate([w_in[:, 4164 + D * b:4164 + D * b + D] for b in BRANCH_ORDER], axis=1)
    up = w_up.transpose(0, 3, 2, 1, 4).reshape(6, 2, P, 4, 256).transpose(0, 2, 1, 3, 4).reshape(6, P, KT, 256)
    weights = np.concatenate([
        _cols(w_in, 1860, 1792), _cols(a["w_mem_kv"][0], 0, 512), _cols(a["w_mem_kv"][0], 512, 512),
        _cols(w_in, 3652, 512), _cols(w_in, 1536, 256), _cols(idx_k, 0, 256), _cols(w_in, 1024, 512),
        _cols(gate, 0, 256 * N_GATE0), _cols(w_in, 0, 512), _cols(w_in, 512, 512), _cols(gate, 256 * N_GATE0, 256 * N_GATE), up,
        _cols(a["w_out"][0], 0, D), _cols(a["peer_w_q"][0], 0, 2048)]).reshape(BLOCKS, P, BLOCK)
    two = lambda x: np.concatenate([x, x])[:, None]
    vec = np.concatenate([
        _vec(a["mix_norm_gain"]), _vec(a["mem_norm_gain"]), _vec(a["gate_bias"][0][list(BRANCH_ORDER)]), _vec(a["rwkv_mu"]),
        _vec(a["rwkv_w0"]), _vec(a["rwkv_a0"]), _vec(a["rwkv_k_k"]), _vec(a["rwkv_k_a"]), _vec(a["rwkv_r_k"]),
        two(a["att_q_gain"][0]), two(a["att_k_gain"][0]), _vec(a["mem_q_gain"]), _vec(a["mem_k_gain"]), _vec(a["ffn_norm_gain"])], axis=1)
    arrays = {
        "x": a["x"][0], "xT": _channel_major(a["x"][0]), "memT": _channel_major(a["mem"][0]), "positions": a["positions"].reshape(S), "const": constants(), "vec": vec,
        "lora": np.concatenate([a["rwkv_w2"][0], a["rwkv_a2"][0]]), "glora": a["rwkv_g2"][0],
        "rows": np.concatenate([a["rwkv_ln_w"][0], a["rwkv_ln_b"][0]]), "ffn_gain": a["ffn_norm_gain"][0],
        "keysT": np.stack([a["peer_key1"][0].T, a["peer_key2"][0].T], axis=1), "weights": weights,
        "experts": np.concatenate([a["peer_u"][0], a["peer_v"][0]], axis=1),
    }
    arrays = {"in_" + k: np.ascontiguousarray(x) for k, x in arrays.items()}
    nc = bacc.Bacc("TRN2", target_bir_lowering=False, num_devices=1)
    t_in = {k[3:]: nc.dram_tensor(k, x.shape, mybir.dt.from_np(x.dtype), kind="ExternalInput").ap()
            for k, x in arrays.items()}
    out = nc.dram_tensor("out", (S, D), F32, kind="ExternalOutput").ap()
    build(nc, t_in, out)
    r = run_bass_kernel_spmd(nc, [arrays], core_ids=[0])
    return r.results[0]["out"].reshape(1, S, D)
```
